# Optimizing a Trainium2 kernel written in Bass

```python
import math
import jax
import jax.numpy as jnp
from jax import lax
import numpy as np

D_MODEL = 1024
BATCH = 1
SEQ = 512
DEPTH = 2

GRID_W = 64
CTX_LEN = 256
Q_BLOCK = 128
ROPE_THETA = 10000.0
EPS = 1e-6

DA_HEADS = 4
DA_HD = 64
DA_VD = 2 * DA_HD
ML_HEADS = 4
ML_QK = 64
ML_V = 128
ML_CHUNK = 64
GQ_HEADS = 8
GQ_KV = 2
GQ_HD = 64
DN_HEADS = 4
DN_HD = 128
DN_CHUNK = 64
DN_CONV = 3
DN_QKV = 3 * DN_HEADS * DN_HD
D_FF = -(-8 * D_MODEL // (3 * 256)) * 256

N_EVEN = (DEPTH + 1) // 2
N_ODD = DEPTH // 2
EVEN_WIDTHS = [DA_HEADS * 2 * DA_HD, DA_HEADS * 2 * DA_HD, DA_HEADS * DA_VD,
               ML_HEADS * ML_QK, ML_HEADS * ML_QK, ML_HEADS * ML_V, ML_HEADS * ML_V, 4 * ML_HEADS]
E_IN = sum(EVEN_WIDTHS)
MIX_EVEN = DA_HEADS * DA_VD + ML_HEADS * ML_V
ODD_WIDTHS = [GQ_HEADS * GQ_HD, GQ_KV * GQ_HD, GQ_KV * GQ_HD, DN_QKV, DN_HEADS * DN_HD, 4 * DN_HEADS]
O_IN = sum(ODD_WIDTHS)
MIX_ODD = GQ_HEADS * GQ_HD + DN_HEADS * DN_HD

kernel_name = 'hybrid_diffusion_backbone'

def rms_norm(x, g):
    xf = x.astype(jnp.float32)
    y = xf * lax.rsqrt(jnp.mean(xf * xf, axis=-1, keepdims=True) + EPS)
    return (y * g.astype(jnp.float32)).astype(x.dtype)

def l2norm(t):
    tf = t.astype(jnp.float32)
    return (tf * lax.rsqrt(jnp.sum(tf * tf, axis=-1, keepdims=True) + EPS)).astype(t.dtype)

def modulate(h, shift, scale):
    return h * (1 + scale) + shift

def split_cols(p, widths):
    return jnp.split(p, np.cumsum(widths)[:-1].tolist(), axis=-1)

def to_heads(t, h):
    b, l, w = t.shape
    return t.reshape(b, l, h, w // h).transpose(0, 2, 1, 3)

def from_heads(t):
    b, h, l, d = t.shape
    return t.transpose(0, 2, 1, 3).reshape(b, l, h * d)

def flip_seq(t):
    return jnp.flip(t, axis=2)

def to_chunks(t, nc, c):
    return jnp.moveaxis(t.reshape(t.shape[:2] + (nc, c) + t.shape[3:]), 2, 0)

def from_chunks(t, l):
    t = jnp.moveaxis(t, 0, 2)
    return t.reshape(t.shape[:2] + (l,) + t.shape[4:])

def axial_rope_tables(n_tok, head_dim):
    rows = n_tok // GRID_W
    quarter = head_dim // 4
    freqs = ROPE_THETA ** (-jnp.arange(quarter, dtype=jnp.float32) / quarter)
    row = jnp.repeat(jnp.arange(rows, dtype=jnp.float32), GRID_W)
    col = jnp.tile(jnp.arange(GRID_W, dtype=jnp.float32), rows)
    ang = jnp.concatenate([row[:, None] * freqs, col[:, None] * freqs], axis=-1)
    return jnp.cos(ang), jnp.sin(ang)

def apply_rope(x, cos, sin):
    shp = x.shape
    q = shp[-1] // 4
    xr = x.reshape(shp[:-1] + (2, 2, q))
    x1, x2 = xr[..., 0, :], xr[..., 1, :]
    c = cos.reshape(cos.shape[0], 2, q)
    s = sin.reshape(sin.shape[0], 2, q)
    out = jnp.stack([x1 * c - x2 * s, x2 * c + x1 * s], axis=-2)
    return out.reshape(shp).astype(x.dtype)

def softmax_mix(q, k, v, coef):
    scale = q.shape[-1] ** -0.5
    s = jnp.einsum('mbhgqd,mbhkd->mbhgqk', q, k).astype(jnp.float32) * scale
    p = jnp.einsum('m,mbhgqk->bhgqk', coef.astype(jnp.float32), jax.nn.softmax(s, axis=-1))
    return jnp.einsum('bhgqk,bhkv->bhgqv', p.astype(v.dtype), v)

def blocked_softmax_mix(q, k, v, coef):
    m, b, hk, g, lq, d = q.shape
    nb = lq // Q_BLOCK
    qb = jnp.moveaxis(q.reshape(m, b, hk, g, nb, Q_BLOCK, d), 4, 0)
    out = lax.map(lambda qi: softmax_mix(qi, k, v, coef), qb)
    return jnp.moveaxis(out, 0, 4).reshape(b, hk, g, lq, v.shape[-1])

def short_conv(x, w):
    kw = w.shape[0]
    pad = (kw - 1) // 2
    y = lax.conv_general_dilated(x, w[:, None, :].astype(x.dtype), window_strides=(1,),
                                 padding=[(pad, kw - 1 - pad)], dimension_numbers=('NWC', 'WIO', 'NWC'),
                                 feature_group_count=x.shape[-1])
    return jax.nn.silu(y)

def mlstm_scan(q, k, v, i_pre, f_pre, state, emit):
    b, h, l, dk = q.shape
    nc = l // ML_CHUNK
    f32 = jnp.float32
    logf = jax.nn.log_sigmoid(f_pre.astype(f32))
    xs = tuple(to_chunks(t, nc, ML_CHUNK) for t in (q.astype(f32), k.astype(f32), v.astype(f32), i_pre.astype(f32), logf))
    causal = jnp.tril(jnp.ones((ML_CHUNK, ML_CHUNK), bool))

    def step(carry, inp):
        c_st, n_st, m_st = carry
        qc, kc, vc, ic, lfc = inp
        bcum = jnp.cumsum(lfc, axis=-1)
        b_end = bcum[..., -1]
        w_end = b_end[..., None] - bcum + ic
        m_new = jnp.maximum(b_end + m_st, jnp.max(w_end, axis=-1))
        decay = jnp.exp(b_end + m_st - m_new)
        w = jnp.exp(w_end - m_new[..., None])
        c_new = decay[..., None, None] * c_st + jnp.einsum('bhs,bhsk,bhsv->bhkv', w, kc, vc)
        n_new = decay[..., None] * n_st + jnp.einsum('bhs,bhsk->bhk', w, kc)
        out = None
        if emit:
            a = bcum + m_st[..., None]
            dmat = jnp.where(causal, bcum[..., :, None] - bcum[..., None, :] + ic[..., None, :], -jnp.inf)
            mt = jnp.maximum(a, jnp.max(dmat, axis=-1))
            inter = jnp.exp(a - mt)
            p = jnp.exp(dmat - mt[..., None]) * jnp.einsum('bhtk,bhsk->bhts', qc, kc)
            num = inter[..., None] * jnp.einsum('bhtk,bhkv->bhtv', qc, c_st) + jnp.einsum('bhts,bhsv->bhtv', p, vc)
            den = inter * jnp.einsum('bhtk,bhk->bht', qc, n_st) + jnp.sum(p, axis=-1)
            out = num / jnp.maximum(jnp.abs(den), jnp.exp(-mt))[..., None]
        return (c_new, n_new, m_new), out

    final, hs = lax.scan(step, state, xs)
    hout = from_chunks(hs, l).astype(v.dtype) if emit else None
    return hout, final

def deltanet_scan(q, k, v, log_decay, beta, state, emit):
    b, h, l, dk = q.shape
    dv = v.shape[-1]
    nc = l // DN_CHUNK
    f32 = jnp.float32
    xs = tuple(to_chunks(t.astype(f32), nc, DN_CHUNK) for t in (q, k, v, log_decay, beta))
    incl = jnp.tril(jnp.ones((DN_CHUNK, DN_CHUNK), bool))
    strict = jnp.tril(jnp.ones((DN_CHUNK, DN_CHUNK), bool), -1)

    def step(s, inp):
        qc, kc, vc, gc, bc = inp
        gcum = jnp.cumsum(gc, axis=-1)
        decay_ts = jnp.exp(jnp.where(incl, gcum[..., :, None] - gcum[..., None, :], -jnp.inf))
        a = jnp.where(strict, bc[..., :, None] * decay_ts * jnp.einsum('bhtk,bhsk->bhts', kc, kc), 0.0)
        gam = jnp.exp(gcum)
        rhs = jnp.concatenate([bc[..., None] * vc, (bc * gam)[..., None] * kc], axis=-1)
        sol = lax.linalg.triangular_solve(a, rhs, left_side=True, lower=True, unit_diagonal=True)
        u = sol[..., :dv] - jnp.einsum('bhtk,bhkv->bhtv', sol[..., dv:], s)
        g_end = gcum[..., -1]
        s_new = jnp.exp(g_end)[..., None, None] * s + jnp.einsum(
            'bhsk,bhsv->bhkv', kc * jnp.exp(g_end[..., None] - gcum)[..., None], u)
        out = None
        if emit:
            attn = jnp.einsum('bhtk,bhsk->bhts', qc, kc) * decay_ts
            out = gam[..., None] * jnp.einsum('bhtk,bhkv->bhtv', qc, s) + jnp.einsum('bhts,bhsv->bhtv', attn, u)
        return s_new, out

    s_fin, outs = lax.scan(step, state, xs)
    o = from_chunks(outs, l).astype(v.dtype) if emit else None
    return o, s_fin

def diff_attention(q_l, k_l, v_l, q_c, k_c, v_c, cos, sin, lam, lam_init, norm_g, emit_ctx):
    def maps(t):
        b, l, _ = t.shape
        return t.reshape(b, l, DA_HEADS, 2, DA_HD).transpose(3, 0, 2, 1, 4)
    ql = apply_rope(maps(q_l), cos, sin)
    kl = apply_rope(maps(k_l), cos, sin)
    qc, kc = maps(q_c), maps(k_c)
    vl, vc = to_heads(v_l, DA_HEADS), to_heads(v_c, DA_HEADS)
    lf = lam.astype(jnp.float32)
    lmb = jnp.exp(jnp.sum(lf[0] * lf[1])) - jnp.exp(jnp.sum(lf[2] * lf[3])) + lam_init
    coef = jnp.stack([jnp.ones_like(lmb), -lmb])
    k_all = jnp.concatenate([kc, kl], axis=3)
    v_all = jnp.concatenate([vc, vl], axis=2)

    def finish(o):
        return from_heads(rms_norm(o[:, :, 0], norm_g) * (1.0 - lam_init))
    y_l = finish(blocked_softmax_mix(ql[:, :, :, None], k_all, v_all, coef))
    y_c = finish(softmax_mix(qc[:, :, :, None], kc, vc, coef)) if emit_ctx else None
    return y_l, y_c

def mlstm_mixer(q_l, k_l, v_l, o_l, g_l, q_c, k_c, v_c, o_c, g_c, gate_bias, norm_g, emit_ctx):
    def prep(q, k, v, g):
        b, l, _ = g.shape
        gates = (g + gate_bias).astype(jnp.float32).reshape(b, l, 4, ML_HEADS).transpose(2, 0, 3, 1)
        return to_heads(q, ML_HEADS), to_heads(k, ML_HEADS) * (ML_QK ** -0.5), to_heads(v, ML_HEADS), gates
    ql, kl, vl, gl = prep(q_l, k_l, v_l, g_l)
    qc, kc, vc, gc = prep(q_c, k_c, v_c, g_c)
    b = ql.shape[0]
    zero = (jnp.zeros((b, ML_HEADS, ML_QK, ML_V), jnp.float32),
            jnp.zeros((b, ML_HEADS, ML_QK), jnp.float32),
            jnp.zeros((b, ML_HEADS), jnp.float32))
    hc_f, st_f = mlstm_scan(qc, kc, vc, gc[0], gc[1], zero, emit_ctx)
    hl_f, _ = mlstm_scan(ql, kl, vl, gl[0], gl[1], st_f, True)
    rc = [flip_seq(t) for t in (qc, kc, vc, gc[2], gc[3])]
    rl = [flip_seq(t) for t in (ql, kl, vl, gl[2], gl[3])]
    hc_b, st_b = mlstm_scan(rc[0], rc[1], rc[2], rc[3], rc[4], zero, emit_ctx)
    hl_b, _ = mlstm_scan(rl[0], rl[1], rl[2], rl[3], rl[4], st_b, True)

    def finish(hsum, o):
        return from_heads(rms_norm(hsum, norm_g)) * jax.nn.sigmoid(o)
    y_l = finish(hl_f + flip_seq(hl_b), o_l)
    y_c = finish(hc_f + flip_seq(hc_b), o_c) if emit_ctx else None
    return y_l, y_c

def gqa_attention(q_l, k_l, v_l, q_c, k_c, v_c, cos, sin, qk_g, emit_ctx):
    def prep(q, k, v):
        return (rms_norm(to_heads(q, GQ_HEADS), qk_g[0]), rms_norm(to_heads(k, GQ_KV), qk_g[1]), to_heads(v, GQ_KV))
    ql, kl, vl = prep(q_l, k_l, v_l)
    qc, kc, vc = prep(q_c, k_c, v_c)
    ql, kl = apply_rope(ql, cos, sin), apply_rope(kl, cos, sin)

    def group(q):
        b, h, l, d = q.shape
        return q.reshape(b, GQ_KV, h // GQ_KV, l, d)[None]

    def finish(o):
        b, hk, g, l, d = o.shape
        return from_heads(o.reshape(b, hk * g, l, d))
    coef = jnp.ones((1,), jnp.float32)
    k_all = jnp.concatenate([kc, kl], axis=2)[None]
    v_all = jnp.concatenate([vc, vl], axis=2)
    y_l = finish(blocked_softmax_mix(group(ql), k_all, v_all, coef))
    y_c = finish(softmax_mix(group(qc), kc[None], vc, coef)) if emit_ctx else None
    return y_l, y_c

def gated_deltanet(qkv_l, z_l, g_l, qkv_c, z_c, g_c, conv_w, a_log, dt_bias, norm_g, emit_ctx):
    def prep(qkv, g):
        q, k, v = jnp.split(short_conv(qkv, conv_w), 3, axis=-1)
        b, l, _ = g.shape
        gates = g.astype(jnp.float32).reshape(b, l, 2, 2, DN_HEADS)
        beta = jax.nn.sigmoid(gates[:, :, :, 0]).transpose(2, 0, 3, 1)
        log_decay = (-jnp.exp(a_log.astype(jnp.float32))
                     * jax.nn.softplus(gates[:, :, :, 1] + dt_bias.astype(jnp.float32))).transpose(2, 0, 3, 1)
        return (l2norm(to_heads(q, DN_HEADS)) * (DN_HD ** -0.5), l2norm(to_heads(k, DN_HEADS)),
                to_heads(v, DN_HEADS), beta, log_decay)
    ql, kl, vl, bl, dl = prep(qkv_l, g_l)
    qc, kc, vc, bc, dc = prep(qkv_c, g_c)
    zero = jnp.zeros((ql.shape[0], DN_HEADS, DN_HD, DN_HD), jnp.float32)
    oc_f, s_f = deltanet_scan(qc, kc, vc, dc[0], bc[0], zero, emit_ctx)
    ol_f, _ = deltanet_scan(ql, kl, vl, dl[0], bl[0], s_f, True)
    rc = [flip_seq(t) for t in (qc, kc, vc, dc[1], bc[1])]
    rl = [flip_seq(t) for t in (ql, kl, vl, dl[1], bl[1])]
    oc_b, s_b = deltanet_scan(rc[0], rc[1], rc[2], rc[3], rc[4], zero, emit_ctx)
    ol_b, _ = deltanet_scan(rl[0], rl[1], rl[2], rl[3], rl[4], s_b, True)

    def finish(o, z):
        return from_heads(rms_norm(o, norm_g)) * jax.nn.silu(z)
    y_l = finish(ol_f + flip_seq(ol_b), z_l)
    y_c = finish(oc_f + flip_seq(oc_b), z_c) if emit_ctx else None
    return y_l, y_c

def mix_even(pl, pc, cos, sin, lam, lam_init, gate_bias, da_g, ml_g, emit_ctx):
    aq_l, ak_l, av_l, bq_l, bk_l, bv_l, bo_l, bg_l = split_cols(pl, EVEN_WIDTHS)
    aq_c, ak_c, av_c, bq_c, bk_c, bv_c, bo_c, bg_c = split_cols(pc, EVEN_WIDTHS)
    ya_l, ya_c = diff_attention(aq_l, ak_l, av_l, aq_c, ak_c, av_c, cos, sin, lam, lam_init, da_g, emit_ctx)
    yb_l, yb_c = mlstm_mixer(bq_l, bk_l, bv_l, bo_l, bg_l, bq_c, bk_c, bv_c, bo_c, bg_c, gate_bias, ml_g, emit_ctx)
    y_l = jnp.concatenate([ya_l, yb_l], axis=-1)
    y_c = jnp.concatenate([ya_c, yb_c], axis=-1) if emit_ctx else None
    return y_l, y_c

def mix_odd(pl, pc, cos, sin, qk_g, conv_w, a_log, dt_bias, dn_g, emit_ctx):
    cq_l, ck_l, cv_l, dqkv_l, dz_l, dg_l = split_cols(pl, ODD_WIDTHS)
    cq_c, ck_c, cv_c, dqkv_c, dz_c, dg_c = split_cols(pc, ODD_WIDTHS)
    yc_l, yc_c = gqa_attention(cq_l, ck_l, cv_l, cq_c, ck_c, cv_c, cos, sin, qk_g, emit_ctx)
    yd_l, yd_c = gated_deltanet(dqkv_l, dz_l, dg_l, dqkv_c, dz_c, dg_c, conv_w, a_log, dt_bias, dn_g, emit_ctx)
    y_l = jnp.concatenate([yc_l, yd_l], axis=-1)
    y_c = jnp.concatenate([yc_c, yd_c], axis=-1) if emit_ctx else None
    return y_l, y_c

def swiglu(h, wg, wu, wd):
    return (jax.nn.silu(h @ wg) * (h @ wu)) @ wd

def setup_inputs(seed: int = 0) -> dict:
    key = jax.random.key(seed)
    ks = iter(jax.random.split(key, 32))
    f32 = jnp.float32

    def nrm(shape, scale):
        return jax.random.normal(next(ks), shape, f32) * scale
    d = D_MODEL
    x = nrm((BATCH, SEQ, d), 1.0)
    c = nrm((BATCH, d), 1.0)
    ctx = nrm((BATCH, CTX_LEN, d), 1.0)
    c_ctx = nrm((d,), 1.0)
    w_ada = nrm((DEPTH, d, 6 * d), 0.5 * d ** -0.5)
    b_ada = nrm((DEPTH, 6 * d), 0.02)
    g_mix = 1.0 + nrm((DEPTH, d), 0.02)
    g_ffn = 1.0 + nrm((DEPTH, d), 0.02)
    w_in_e = nrm((N_EVEN, d, E_IN), d ** -0.5)
    i_bias = nrm((N_EVEN, 2, ML_HEADS), 0.1)
    f_bias = jnp.linspace(3.0, 6.0, ML_HEADS, dtype=f32) + nrm((N_EVEN, 2, ML_HEADS), 0.1)
    b_gate_e = jnp.stack([i_bias, f_bias], axis=2).reshape(N_EVEN, 4 * ML_HEADS)
    da_lam = nrm((N_EVEN, 4, DA_HD), 0.1)
    da_norm_g = 1.0 + nrm((N_EVEN, DA_VD), 0.02)
    ml_norm_g = 1.0 + nrm((N_EVEN, ML_V), 0.02)
    w_out_e = nrm((N_EVEN, MIX_EVEN, d), MIX_EVEN ** -0.5)
    w_in_o = nrm((N_ODD, d, O_IN), d ** -0.5)
    qk_norm_g = 1.0 + nrm((N_ODD, 2, GQ_HD), 0.02)
    dn_conv = nrm((N_ODD, DN_CONV, DN_QKV), DN_CONV ** -0.5)
    dn_a_log = jnp.log(jnp.linspace(1.0, 16.0, DN_HEADS, dtype=f32)) + nrm((N_ODD, 2, DN_HEADS), 0.05)
    dt = jnp.exp(jax.random.uniform(next(ks), (N_ODD, 2, DN_HEADS), f32, math.log(1e-3), math.log(1e-1)))
    dn_dt_bias = dt + jnp.log(-jnp.expm1(-dt))
    dn_norm_g = 1.0 + nrm((N_ODD, DN_HD), 0.02)
    w_out_o = nrm((N_ODD, MIX_ODD, d), MIX_ODD ** -0.5)
    w_gate = nrm((DEPTH, d, D_FF), d ** -0.5)
    w_up = nrm((DEPTH, d, D_FF), d ** -0.5)
    w_down = nrm((DEPTH, D_FF, d), D_FF ** -0.5)
    g_final = 1.0 + nrm((d,), 0.02)
    return {'x': x, 'c': c, 'ctx': ctx, 'c_ctx': c_ctx, 'w_ada': w_ada, 'b_ada': b_ada,
            'g_mix': g_mix, 'g_ffn': g_ffn, 'w_in_e': w_in_e, 'b_gate_e': b_gate_e, 'da_lam': da_lam,
            'da_norm_g': da_norm_g, 'ml_norm_g': ml_norm_g, 'w_out_e': w_out_e, 'w_in_o': w_in_o,
            'qk_norm_g': qk_norm_g, 'dn_conv': dn_conv, 'dn_a_log': dn_a_log, 'dn_dt_bias': dn_dt_bias,
            'dn_norm_g': dn_norm_g, 'w_out_o': w_out_o, 'w_gate': w_gate, 'w_up': w_up, 'w_down': w_down,
            'g_final': g_final}

def reference(x, c, ctx, c_ctx, w_ada, b_ada, g_mix, g_ffn, w_in_e, b_gate_e, da_lam, da_norm_g, ml_norm_g,
              w_out_e, w_in_o, qk_norm_g, dn_conv, dn_a_log, dn_dt_bias, dn_norm_g, w_out_o, w_gate, w_up,
              w_down, g_final):
    n_tok = x.shape[1]
    cos, sin = axial_rope_tables(n_tok, DA_HD)
    silu_c = jax.nn.silu(c)
    silu_cc = jax.nn.silu(c_ctx)
    xl, xc = x, ctx
    for layer in range(DEPTH):
        emit_ctx = layer < DEPTH - 1
        mod_l = (silu_c @ w_ada[layer] + b_ada[layer])[:, None, :]
        mod_c = silu_cc @ w_ada[layer] + b_ada[layer]
        sh1, sc1, ga1, sh2, sc2, ga2 = jnp.split(mod_l, 6, axis=-1)
        sh1c, sc1c, ga1c, sh2c, sc2c, ga2c = jnp.split(mod_c, 6, axis=-1)
        hl = modulate(rms_norm(xl, g_mix[layer]), sh1, sc1)
        hc = modulate(rms_norm(xc, g_mix[layer]), sh1c, sc1c)
        if layer % 2 == 0:
            e = layer // 2
            lam_init = 0.8 - 0.6 * math.exp(-0.3 * layer)
            yl, yc = mix_even(hl @ w_in_e[e], hc @ w_in_e[e], cos, sin, da_lam[e], lam_init, b_gate_e[e],
                              da_norm_g[e], ml_norm_g[e], emit_ctx)
            w_out = w_out_e[e]
        else:
            o = layer // 2
            yl, yc = mix_odd(hl @ w_in_o[o], hc @ w_in_o[o], cos, sin, qk_norm_g[o], dn_conv[o], dn_a_log[o],
                             dn_dt_bias[o], dn_norm_g[o], emit_ctx)
            w_out = w_out_o[o]
        xl = xl + ga1 * (yl @ w_out)
        xl = xl + ga2 * swiglu(modulate(rms_norm(xl, g_ffn[layer]), sh2, sc2), w_gate[layer], w_up[layer], w_down[layer])
        if emit_ctx:
            xc = xc + ga1c * (yc @ w_out)
            xc = xc + ga2c * swiglu(modulate(rms_norm(xc, g_ffn[layer]), sh2c, sc2c), w_gate[layer], w_up[layer], w_down[layer])
    return rms_norm(xl, g_final)


_drawn_inputs = setup_inputs


def setup_inputs(seed=0):
    import zlib

    import numpy as np

    out = dict(_drawn_inputs(seed))
    spreads = {}
    factors = {'g_mix': 6.634,
     'g_ffn': 6.604,
     'da_lam': 4.021,
     'da_norm_g': 8.0,
     'ml_norm_g': 8.0,
     'qk_norm_g': 8.0,
     'dn_norm_g': 8.0,
     'g_final': 2.801}
    for name, (base, spread) in spreads.items():
        noise = np.random.default_rng([zlib.crc32(name.encode()), seed]).standard_normal(out[name].shape)
        drawn = base * np.exp(spread * noise) if base else spread * noise
        out[name] = jnp.asarray(drawn.astype(out[name].dtype))
    for name, factor in factors.items():
        out[name] = (out[name] * factor).astype(out[name].dtype)
    return out
```

```python
from contextlib import ExitStack

import numpy as np

import concourse.bass as bass
from concourse import mybir

F32 = mybir.dt.float32
BF16 = mybir.dt.bfloat16
ACT = mybir.ActivationFunctionType
ALU = mybir.AluOpType
AX_X = mybir.AxisListType.X

P = 128
D = 1024
KD = D // P
CTX, LAT = 256, 512
T = CTX + LAT
NT = T // P
DFF = 2816
FC = DFF // P
GRID_W = 64
EPS = 1e-6
HEADS = 4
E_IN, O_IN = 3088, 2832
E_GATES, O_GATES = 3072, 2816
LAM_INIT = 0.2
BANK = 512
SLOTS = 4
GROW = 36
NEG = -1e30
LEVELS = 7
DAQ, DAK, DAV, MLQ, MLK, MLV, MLO = 0, 4, 8, 12, 14, 16, 20
CQ, CK, CV, DNQ, DNK, DNV, DNZ = 0, 4, 5, 6, 10, 14, 18
G_MIX, G_FFN, G_FINAL, V_C, V_CCTX, G_DA, G_ML, G_DN, G_Q, G_K, CONV = 0, 16, 32, 40, 48, 56, 57, 58, 59, 60, 61
NVEC = CONV + 36
SH1, SC1, GA1, SH2, SC2, GA2 = 0, 8, 16, 24, 32, 40

C_ID, C_ONES, C_PERM, C_BLK, C_RST = 0, 128, 256, 384, 512
NCF = 640
B_ID, B_INCL, B_STRICT, B_LEVEL = 0, 128, 384, 640
NCB = B_LEVEL + LEVELS * 2 * P


def constant_tables():
    f = np.zeros((P, NCF), np.float32)
    i = np.arange(P)
    f[:, C_ID:C_ID + P] = np.eye(P)
    f[:, C_ONES:C_ONES + P] = 1.0
    f[i, C_PERM + (i ^ 16)] = 1.0
    f[:, C_BLK:C_BLK + P] = i[:, None] // 64 == i[None, :] // 64
    quarter = 16
    freqs = 10000.0 ** (-np.arange(quarter, dtype=np.float32) / np.float32(quarter))
    t = np.arange(LAT)
    pos = np.stack([t // GRID_W, t % GRID_W]).astype(np.float32)
    axis, second, idx = (i % 64) // 32, (i % 32) // 16, i % 16
    ang = pos[axis] * freqs.astype(np.float32)[idx][:, None]
    rot = np.concatenate([np.cos(ang), np.sin(ang) * np.where(second == 1, 1.0, -1.0)[:, None]], 1)
    f[0:32, C_RST:C_RST + P] = i != 0
    f[32:, C_RST:C_RST + P] = i != P - 1
    b = np.zeros((P, NCB), np.float32)
    b[:, B_ID:B_ID + P] = np.eye(P)
    s, q = i[:, None], i[None, :]
    for d in range(2):
        lo, hi = (s, q) if d == 0 else (q, s)
        b[:, B_INCL + d * P:B_INCL + (d + 1) * P] = np.where(lo <= hi, 0.0, NEG)
        b[:, B_STRICT + d * P:B_STRICT + (d + 1) * P] = np.where(lo < hi, 0.0, NEG)
        for k in range(LEVELS):
            w = 1 << k
            at = B_LEVEL + (k * 2 + d) * P
            b[:, at:at + P] = -1.0 * ((hi // w % 2 == 1) & (lo // w == hi // w - 1))
    return f, (b.view(np.uint32) >> 16).astype(np.uint16), rot.astype(np.float32)


STREAM = [("ada0", 8, 2), ("proj0", 12, 2), ("adb0", 16, 2), ("ada1", 24, 2), ("out0", 4, 2), ("up0", 22, 2), ("down0", 16, 1),
          ("proj1", 11, 2), ("out1", 4, 2), ("up1", 22, 2), ("down1", 16, 1)]


def stream_plan():
    plan, used_at, load, done = {}, [], 0, 0
    for name, n, per in STREAM:
        plan[name] = (load, n, per, done)
        used_at += [done + per * (j + 1) for j in range(n)]
        load += n
        done += per * n
    return plan, used_at


PLAN, USED_AT = stream_plan()


def backbone(nc, x, c, ctx_tok, c_ctx, w_ada, b_ada, g_mix, g_ffn, w_in_e, b_gate_e, da_lam, da_norm_g, ml_norm_g,
             w_out_e, w_in_o, qk_norm_g, dn_conv, dn_a_log, dn_dt_bias, dn_norm_g, w_out_o, w_gate, w_up, w_down,
             g_final, const_f, const_b, rotary, out):
    stack = ExitStack()
    with stack:
        def sb(name, shape, dt=F32):
            return stack.enter_context(nc.sbuf_tensor(name, shape, dt))

        named = {}

        def sem(name):
            if name not in named:
                named[name] = stack.enter_context(nc.semaphore(name))
            return named[name]

        xT = sb("xT", [P, KD, T])
        hT = sb("hT", [P, KD, T])
        proj = sb("proj", [P, 24, T])
        tok = sb("tok", [P, 10 * T])
        ring = sb("ring", [P, SLOTS, 2048])
        cf = sb("cf", [P, NCF])
        cb_bits = sb("cb_bits", [P, NCB], mybir.dt.uint16)
        cb = cb_bits[:].bitcast(BF16)
        sq = sb("sq", [P, 2, T])
        rs = sb("rs", [P, 2, T])
        vec_a = sb("vec_a", [P, 96])
        vec_b = sb("vec_b", [P, NVEC])
        modT = sb("modT", [P, 2, 48, 2])
        gmT = sb("gmT", [P, 2, 2, KD, 2])
        silu_c = sb("silu_c", [P, KD, 2])
        gate_in = sb("gate_in", [P, 2, KD, 16])
        gate_b = sb("gate_b", [GROW, 8])
        cols = sb("cols", [P, 4, NT, 8])
        endr = sb("endr", [GROW, 6, 8])
        endx = sb("endx", [GROW, NT, GROW])
        endb = sb("endb", [P, NT, 8])
        small = sb("small", [P, 32])
        PS = stack.enter_context(nc.psum_tensor("PS", [P, 8 * BANK], F32))

        ident, ones, perm, blk = (cf[:, a:a + P] for a in (C_ID, C_ONES, C_PERM, C_BLK))
        rot_at = [proj[:, b:b + 2, :].rearrange("p a t -> p (a t)")[:, 0:2 * LAT] for b in (9, 16)]
        ident_b = cb[:, B_ID:B_ID + P]
        incl = [cb[:, B_INCL + d * P:B_INCL + (d + 1) * P] for d in range(2)]
        strict = [cb[:, B_STRICT + d * P:B_STRICT + (d + 1) * P] for d in range(2)]
        tok_e = tok[:, 0:NT * 1280].rearrange("p (t n) -> p t n", t=NT)
        tok_o = tok[:, 0:NT * 1152].rearrange("p (t n) -> p t n", t=NT)
        tok_free = tok[:, NT * 1152:NT * 1152 + T]
        x_tok = proj[:, 0:8, :].rearrange("p a b -> p (a b)").rearrange("p (t n) -> p t n", t=NT)
        out_tok = proj[:, 0:6, :].rearrange("p a b -> p (a b)")[:, 0:4 * D].rearrange("p (t n) -> p t n", t=4)
        vec_rows = proj[:, 8, 0:256].rearrange("p (a n) -> p a n", a=2)
        gate_w = [proj[:, b, 0:KD * 2 * GROW].rearrange("p (k a n) -> p k a n", k=KD, a=2) for b in (8, 15)]
        lam_in = proj[:, 10, 0:256].rearrange("p (a n) -> p a n", a=4)
        lam_tmp = proj[:, 10, 256:384].rearrange("p (a n) -> p a n", a=2)

        def bank(b, n=BANK):
            return PS[:, b * BANK:b * BANK + n]

        def ps(b, lo, hi):
            return PS[:, b * BANK + lo:b * BANK + hi]

        def sel(d, j):
            r = 32 * d + j
            return cf[0:GROW, C_ID + r:C_ID + r + 1].to_broadcast([GROW, P])

        def slot(i):
            return proj[:, i, :]

        class Att:
            def __init__(self, layer):
                self.layer = layer
                if layer == 0:
                    self.maps, self.vd = 2, P
                    self.tiles = [(h, q) for h in range(HEADS) for q in range(NT)]
                    self.E = [[slot(8), slot(9)], [slot(10), slot(11)]]
                    self.PT = [slot(18), slot(19)]
                else:
                    self.maps, self.vd = 1, 64
                    self.tiles = [(h, q) for h in range(8) for q in range(2, NT)]
                    self.E = [[slot(15)], [slot(16)]]
                    self.PT = [slot(17), tok_free]

            def keys(self, i):
                return T if self.tiles[i][1] >= 2 else CTX

            def q(self, i, m):
                h, q = self.tiles[i]
                if self.layer == 0:
                    return proj[64 * m:64 * m + 64, DAQ + h, P * q:P * q + P]
                r = 64 * (h % 2)
                return proj[r:r + 64, CQ + h // 2, P * q:P * q + P]

            def k(self, i, m, lo, hi):
                h, _ = self.tiles[i]
                if self.layer == 0:
                    return proj[64 * m:64 * m + 64, DAK + h, lo:hi]
                r = 64 * (h % 2)
                return proj[r:r + 64, 22 + h // 4, lo:hi]

            def v(self, i, kt):
                h, _ = self.tiles[i]
                if self.layer == 0:
                    return tok_e[:, kt, P * h:P * h + P]
                return tok_o[:, kt, 1024 + 64 * (h // 4):1024 + 64 * (h // 4) + 64]

            def rows(self, i):
                h, _ = self.tiles[i]
                return (0, P) if self.layer == 0 else (64 * (h % 2), 64 * (h % 2) + 64)

            def y(self, i):
                h, q = self.tiles[i]
                lo, hi = self.rows(i)
                block_ = hT[lo:hi, h if self.layer == 0 else h // 2, :]
                return block_[:, P * q:P * q + P] if q < 2 else block_[:, CTX + q - 2:T:LAT // P]

        def head_norm_items(stage):
            if stage == "da":
                return [(hT[:, h, :], ones, 1.0 / P, small[:, 4:5], hT[:, h, :], T) for h in range(HEADS)]
            if stage == "ml":
                return [(hT[:, 4 + h, :], ones, 1.0 / P, vec_b[:, G_ML:G_ML + 1], hT[:, 4 + h, :], T) for h in range(HEADS)]
            if stage == "qk":
                its = [(proj[:, CQ + b, CTX:T], blk, 1.0 / 64, vec_b[:, G_Q:G_Q + 1], proj[:, CQ + b, CTX:T], LAT) for b in range(4)]
                return its + [(proj[:, CK, :], blk, 1.0 / 64, vec_b[:, G_K:G_K + 1], proj[:, CK, :], T)]
            if stage == "l2":
                return [(proj[:, b, :], ones, 1.0, P ** -0.5 if b < DNK else 1.0, proj[:, b, :], T) for b in range(DNQ, DNV)]
            return [(hT[:, 4 + h, CTX:T], ones, 1.0 / P, vec_b[:, G_DN:G_DN + 1], hT[:, 4 + h, CTX:T], LAT) for h in range(HEADS)]

        def transposes(stage):
            if stage == "even":
                its = []
                for t in range(NT):
                    for first, n, at in ((DAV, 4, 0), (MLV, 4, 512), (MLK, 2, 1024)):
                        its.append(([proj[:, first + j, P * t:P * t + P] for j in range(n)], tok_e[:, t, at:at + P * n]))
                return its
            its = []
            for t in range(NT):
                for first, n, at in ((DNV, 4, 0), (DNK, 4, 512), (CV, 1, 1024)):
                    its.append(([proj[:, first + j, P * t:P * t + P] for j in range(n)], tok_o[:, t, at:at + P * n]))
            return its

        ROPE = {0: [DAQ + j for j in range(8)], 1: [CQ + j for j in range(5)]}

        ORDER = [[0, 1, 2, 3, 4, 5], [1, 0, 5, 4, 3, 2]]
        rowI, rowF = proj[0:GROW, 16, :], proj[0:GROW, 17, :]
        er = [proj[0:GROW, i, :] for i in range(8)]
        e_logf, e_m, e_b, e_ib, e_A, e_inter, e_em, e_t = er
        o_rst = proj[0:GROW, 15, :]
        o_rowI, o_rowF = proj[0:GROW, 5, :], proj[0:GROW, 14, :]
        o_g, o_gb, o_eg, o_t = sq[0:GROW, 0, :], sq[0:GROW, 1, :], rs[0:GROW, 0, :], rs[0:GROW, 1, :]
        pexp, pm, qt, den = slot(8), slot(9), slot(10), slot(11)
        cst = proj[:, 18:20, :].rearrange("p a b -> p (a b)").rearrange("p (c n) -> p c n", c=NT)
        kw = sq[:, 0, 0:NT * 64].rearrange("p (c n) -> p c n", c=NT)
        runA = proj[:, 0:6, :].rearrange("p a b -> p (a b)")
        runB = proj[:, 14:18, :].rearrange("p a b -> p (a b)")
        runC = proj[:, 22:24, :].rearrange("p a b -> p (a b)")
        bufs = [r[:, 512 * i:512 * i + 512] for r, n in ((runA, 9), (runB, 6), (runC, 3)) for i in range(n)]
        AT, LV, X, XT, Y, ATTN, KB, VB, WT, KDC = bufs[0], bufs[1:8], bufs[8], bufs[9], bufs[10], bufs[11], bufs[12], bufs[13], bufs[14], bufs[15]
        U, ST = bufs[16], bufs[17]
        QG = tok_free[:, 0:512]
        UNITS = [(d, i, c) for d in range(2) for i, c in enumerate(ORDER[d])]

        resets = cf[0:GROW, C_RST:C_RST + P].unsqueeze(1).to_broadcast([GROW, NT, P])

        def h4(ap):
            return ap.rearrange("p (h n) -> p h n", h=4)

        weights = {"proj0": w_in_e[0], "proj1": w_in_o[0], "out0": w_out_e[0], "out1": w_out_o[0]}
        weights["ada0"], weights["adb0"], weights["ada1"] = w_ada[0][:, 0:16 * P], w_ada[0][:, 16 * P:], w_ada[1]

        def segments(c0):
            return [(0, 512), (512, T)] if c0 == 0 else [(c0, T)]

        block = stack.enter_context(nc.Block())

        @block.sync
        def _(sp):
            sp.dma_start(cf[:], const_f).then_inc(sem("const_in"), 16)
            sp.dma_start(vec_rows[0:96, 0, :], b_ada.rearrange("l (m p) -> (l m) p", p=P)).then_inc(sem("vec_in"), 16)
            for at, src in ((G_MIX, g_mix.rearrange("l (m p) -> (l m) p", p=P)), (G_FFN, g_ffn.rearrange("l (m p) -> (l m) p", p=P)),
                            (G_FINAL, g_final.rearrange("(m p) -> m p", p=P)), (V_C, c.rearrange("b (m p) -> (b m) p", p=P)),
                            (V_CCTX, c_ctx.rearrange("(m p) -> m p", p=P)), (G_DA, da_norm_g), (G_ML, ml_norm_g), (G_DN, dn_norm_g),
                            (CONV, dn_conv.rearrange("o t (m p) -> (o t m) p", p=P))):
                sp.dma_start(vec_rows[at:at + src.shape[0], 1, :], src).then_inc(sem("vec_in"), 16)
            for half in range(2):
                sp.dma_start(vec_rows[G_Q:G_Q + 2, 1, 64 * half:64 * half + 64], qk_norm_g[0]).then_inc(sem("vec_in"), 16)
            sp.dma_start(x_tok[:, 0:2, :], ctx_tok[0].rearrange("(t p) d -> p t d", p=P)).then_inc(sem("tok_in"), 16)
            sp.dma_start(x_tok[:, 2:6, :], x[0].rearrange("(t p) d -> p t d", p=P)).then_inc(sem("tok_in"), 16)
            sp.dma_start(cb_bits[:], const_b).then_inc(sem("const_in"), 16)
            for l, w, at in ((0, w_in_e, E_GATES), (1, w_in_o, O_GATES)):
                sp.dma_start(gate_in[:, l], w[0].rearrange("(k p) n -> p k n", p=P)[:, :, at:at + 16]).then_inc(sem("gates_in"), 16)
            sp.dma_start(lam_in, da_lam.partition_broadcast(P).rearrange("p o a n -> p (o a) n")).then_inc(sem("gates_in"), 16)
            sp.wait_ge(sem("cleared"), 1)
            col = lambda ap: ap.rearrange("(p q) -> p q", q=1)
            for d in range(2):
                r = slice(32 * d, 32 * d + 4)
                sp.dma_start(gate_b[r, 0:1], col(b_gate_e[0, 8 * d:8 * d + 4])).then_inc(sem("gates_in"), 16)
                sp.dma_start(gate_b[r, 1:2], col(b_gate_e[0, 8 * d + 4:8 * d + 8])).then_inc(sem("gates_in"), 16)
                sp.dma_start(gate_b[r, 2:3], col(dn_dt_bias[0, d])).then_inc(sem("gates_in"), 16)
                sp.dma_start(gate_b[r, 3:4], col(dn_a_log[0, d])).then_inc(sem("gates_in"), 16)

            def load(stage, k, s):
                if stage[:-1] == "down":
                    n, half = k
                    src = w_down[int(stage[-1])].rearrange("(k p) n -> p k n", p=P)[:, 11 * half:11 * half + 11, bass.ds(128 * n, 128)]
                    dst = ring[:, s, 0:11 * 128].rearrange("p (k n) -> p k n", k=11)
                elif stage[:-1] == "up":
                    n, which = k
                    src = (w_gate, w_up)[which][int(stage[-1])].rearrange("(k p) n -> p k n", p=P)[:, :, bass.ds(256 * n, 256)]
                    dst = ring[:, s, :].rearrange("p (k n) -> p k n", k=KD)
                else:
                    src = weights[stage].rearrange("(k p) n -> p k n", p=P)[:, :, bass.ds(256 * k, 256)]
                    dst = ring[:, s, :].rearrange("p (k n) -> p k n", k=KD)
                sp.dma_start(dst, src).then_inc(sem(f"weights_in{s}"), 16)

            def part(stage, i, k):
                return (2 * i + k // 2, k % 2) if stage[:-1] in ("up", "down") else 4 * i + k

            def stream(stage):
                j0, n, per, done = PLAN[stage]
                for k in range(min(4, n)):
                    if j0 + k >= SLOTS:
                        sp.wait_ge(sem("products"), USED_AT[j0 + k - SLOTS])
                    load(stage, part(stage, 0, k), (j0 + k) % SLOTS)
                if n // 4 > 1:
                    with sp.Fori(1, n // 4) as i:
                        for k in range(4):
                            sp.wait_ge(sem("products"), 4 * per * i + (done + per * (k - 3)))
                            load(stage, part(stage, i, k), (j0 + k) % SLOTS)
                for k in range(max(4, n // 4 * 4), n):
                    sp.wait_ge(sem("products"), USED_AT[j0 + k - SLOTS])
                    load(stage, part(stage, n // 4, k % 4), (j0 + k) % SLOTS)

            for stage, _, _ in STREAM:
                stream(stage)
                if stage[:-1] == "proj":
                    layer = int(stage[-1])
                    sp.wait_ge(sem("moved_odd" if layer else "moved_even"), 3 * NT)
                    sp.dma_start(rot_at[layer], rotary).then_inc(sem("rotary_in"), 16)
                if stage == "proj1":
                    sp.wait_ge(sem("rope_done1"), 5)
                    for g in range(2):
                        for half in range(2):
                            sp.dma_start(proj[64 * half:64 * half + 64, 22 + g, :], proj[64 * g:64 * g + 64, CK, :]).then_inc(sem("keys_spread"), 16)
            sp.wait_ge(sem("out_moved"), 8)
            sp.dma_start(out[0].rearrange("(t p) d -> p t d", p=P), out_tok).then_inc(sem("stored"), 16)
            sp.wait_ge(sem("stored"), 16)

        @block.gpsimd
        def _(pool):
            nc.gpsimd.memset(gate_b[:], 0.0).then_inc(sem("cleared"), 1)
            for layer in range(2):
                pool.wait_ge(sem("moved_odd" if layer else "moved_even"), 3 * NT)
                pool.wait_ge(sem("gates_in"), 16 * 11)
                nc.gpsimd.memset(gate_w[layer], 0.0).then_inc(sem("gate_w"), 1)
                pool.wait_ge(sem("gate_w"), 5 * layer + 1)
                for kind in range(2):
                    for d in range(2):
                        at = 8 * d + 4 * kind
                        nc.gpsimd.tensor_copy(gate_w[layer][:, :, kind, 32 * d:32 * d + 4], gate_in[:, layer, :, at:at + 4]).then_inc(sem("gate_w"), 1)

            for u, (d, i, c) in enumerate(UNITS):
                if u == 0:
                    pool.wait_ge(sem("dn_cols"), 1)
                if u >= 1:
                    pool.wait_ge(sem("dn_state"), u)
                    pool.wait_ge(sem("dn_u"), u)
                if u == 0:
                    pool.wait_ge(sem("moved_odd"), 3 * NT)
                    pool.wait_ge(sem("att_y1"), 32)
                r = slice(4 * d, 4 * d + 4)

                def by_col(dst, at, which):
                    return nc.gpsimd.tensor_tensor(h4(dst), tok_o[:, c, at:at + 512].rearrange("p (h n) -> p h n", h=4),
                                                   cols[:, which, c, r].unsqueeze(2).to_broadcast([P, 4, P]), ALU.mult)
                by_col(VB, 0, 0).then_inc(sem("dn_scaled"), 1)
                by_col(KB, 512, 1).then_inc(sem("dn_scaled"), 1)
                by_col(KDC, 512, 2).then_inc(sem("dn_scaled"), 1)
                pool.wait_ge(sem("dn_at"), u + 1)
                for k in range(LEVELS):
                    at = B_LEVEL + (k * 2 + d) * P
                    nc.gpsimd.tensor_tensor(h4(LV[k]), h4(AT), cb[:, at:at + P].unsqueeze(1).to_broadcast([P, 4, P]),
                                            ALU.mult).then_inc(sem("dn_level"), 1)

        @block.tensor
        def _(pe):
            mm, tr = nc.tensor.matmul, nc.tensor.transpose
            pe.wait_ge(sem("const_in"), 32)
            pe.wait_ge(sem("vec_in"), 16 * 12)
            tr(ps(0, 0, 96), vec_rows[0:96, 0, :], ident[0:96, 0:96]).then_inc(sem("vec_turned"), 1)
            tr(ps(1, 0, NVEC), vec_rows[0:NVEC, 1, :], ident[0:NVEC, 0:NVEC]).then_inc(sem("vec_turned"), 1)
            pe.wait_ge(sem("tok_in"), 32)
            for k in range(KD):
                if k >= 2:
                    pe.wait_ge(sem("x_moved"), k - 1)
                for t in range(NT):
                    last = tr(ps(2 + 2 * (k % 2), P * t, P * t + P), x_tok[:, t, P * k:P * k + P], ident)
                last.then_inc(sem("x_turned"), 1)

            def arrived(j, i=None):
                v = 16 * (j // SLOTS + 1)
                pe.wait_ge(sem(f"weights_in{j % SLOTS}"), v if i is None else 16 * i + v)

            def wslot(j, k, half):
                at = 256 * k + 128 * half
                return ring[:, j % SLOTS, at:at + 128]

            def looped(stage, body, peeled):
                j0, n, _, _ = PLAN[stage]
                for k in range(4 * peeled):
                    arrived(j0 + k)
                    body(k, 0)
                if n // 4 > 1:
                    with pe.Fori(peeled, n // 4) as i:
                        for k in range(4):
                            arrived(j0 + k, i)
                            body(k, i)
                for k in range(max(n // 4, peeled) * 4, n):
                    arrived(j0 + k)
                    body(k % 4, k // 4)

            pe.wait_ge(sem("silu_c"), 1)

            def ada_load(j, column):
                arrived(j)
                for half in range(2):
                    for kk in range(KD):
                        last = mm(ps(6, column + 2 * half, column + 2 * half + 2), wslot(j, kk, half), silu_c[:, kk, :],
                                  start=kk == 0, stop=kk == KD - 1)
                    last.then_inc(sem("products"), 1)

            for j in range(8):
                ada_load(PLAN["ada0"][0] + j, 4 * j)

            def norm_sums(tag, c0):
                for k in range(KD):
                    pe.wait_ge(sem("squared"), norm_no[0] * KD + k + 1)
                    for lo, hi in segments(c0):
                        last = mm(PS[:, lo - c0:hi - c0], ones, sq[:, k % 2, lo:hi], start=k == 0, stop=k == KD - 1)
                    last.then_inc(sem("squares_summed"), 1)
                norm_no[0] += 1

            norm_no = [0]

            def project(stage, c0, operand, free, per=1):
                j0, _, _, _ = PLAN[stage]

                def body(k, i):
                    for half in range(2):
                        b = 2 * k + half
                        a = 2 * (b % 4)
                        if isinstance(i, int):
                            if 8 * i + b >= 4:
                                pe.wait_ge(sem(free), per * (8 * i + b - 3))
                        else:
                            pe.wait_ge(sem(free), 8 * per * i + per * (b - 3))
                        for kk in range(KD):
                            for lo, hi in segments(c0):
                                last = mm(ps(a, lo - c0, hi - c0), wslot(j0 + k, kk, half), operand[:, kk, lo:hi],
                                          start=kk == 0, stop=kk == KD - 1)
                        last.then_inc(sem("products"), 1)
                looped(stage, body, 1)

            def gates(layer):
                pe.wait_ge(sem("gate_w"), 5 * (layer + 1))
                for kind in range(2):
                    for kk in range(KD):
                        for lo, hi in segments(0):
                            last = mm(PS[0:GROW, (4 + 2 * kind) * BANK + lo:(4 + 2 * kind) * BANK + hi], gate_w[layer][:, kk, kind, :],
                                      hT[:, kk, lo:hi], start=kk == 0, stop=kk == KD - 1)
                    last.then_inc(sem("gate_rows"), 1)

            def turn(stage, first_wait):
                for i, (srcs, _) in enumerate(transposes(stage)):
                    if i >= 4:
                        pe.wait_ge(sem(f"moved_{stage}"), i - 3)
                    for j, src in enumerate(srcs):
                        last = tr(ps(i % 4, P * j, P * j + P), src, ident)
                    last.then_inc(sem(f"turned_{stage}"), 1)

            def head_norm_sums(stage):
                for i, (_, mat, _, _, _, n) in enumerate(head_norm_items(stage)):
                    pe.wait_ge(sem(f"hsq_{stage}"), i + 1)
                    if i >= 2:
                        pe.wait_ge(sem(f"hms_{stage}"), i - 1)
                    for lo, hi in ((0, 512), (512, n)):
                        if hi > lo:
                            last = mm(ps(2 * (i % 2), lo, hi), mat, sq[:, i % 2, lo:hi], start=True, stop=True)
                    last.then_inc(sem(f"hsum_{stage}"), 1)

            def rope(layer):
                for i, b in enumerate(ROPE[layer]):
                    if i >= 2:
                        pe.wait_ge(sem(f"rope_done{layer}"), i - 1)
                    mm(ps(4 + i % 2, 0, LAT), perm, proj[:, b, CTX:T], start=True, stop=True).then_inc(sem(f"rope_swapped{layer}"), 1)

            def attention(layer):
                a = Att(layer)
                n = len(a.tiles)

                def scores(i):
                    for m in range(a.maps):
                        b = 2 * m if a.maps == 2 else 2 * (i % 2)
                        if a.maps == 2 and i >= 1:
                            pe.wait_ge(sem(f"att_exp{layer}"), 2 * (i - 1) + m + 1)
                        if a.maps == 1 and i >= 2:
                            pe.wait_ge(sem(f"att_exp{layer}"), i - 1)
                        nk = a.keys(i)
                        for lo, hi in ((0, min(512, nk)), (512, nk)):
                            if hi > lo:
                                last = mm(ps(b, lo, hi), a.q(i, m), a.k(i, m, lo, hi), start=True, stop=True)
                        last.then_inc(sem(f"att_scores{layer}"), 1)

                def values(i):
                    nk = a.keys(i) // P
                    pe.wait_ge(sem(f"att_pt{layer}"), i + 1)
                    if i >= 1:
                        pe.wait_ge(sem(f"att_y{layer}"), i)
                    lo, hi = a.rows(i)
                    for kt in range(nk):
                        last = mm(PS[lo:hi, 7 * BANK:7 * BANK + P], a.v(i, kt), a.PT[i % 2][:, P * kt:P * kt + P],
                                  start=kt == 0, stop=kt == nk - 1)
                    last.then_inc(sem(f"att_out{layer}"), 1)

                scores(0)
                for i in range(n):
                    if i + 1 < n:
                        scores(i + 1)
                    if i >= 1:
                        values(i - 1)
                    if layer == 0 and i < 20:
                        for j in range(2 * i, 2 * i + 2):
                            ada_load(PLAN["adb0"][0] + j, 32 + 4 * j)
                    nk = a.keys(i) // P
                    pe.wait_ge(sem(f"att_probs{layer}"), i + 1)
                    if i >= 1:
                        pe.wait_ge(sem(f"att_pt{layer}"), i)
                    for kt in range(nk):
                        last = tr(ps(4, P * kt, P * kt + P), a.E[i % 2][0][:, P * kt:P * kt + P], ident)
                    last.then_inc(sem(f"att_turned{layer}"), 1)
                values(n - 1)

            def row_columns(layer, rows):
                pe.wait_ge(sem(f"rows_ready{layer}"), 1)
                for w, row in enumerate(rows):
                    for ch in range(NT):
                        last = tr(PS[:, w * BANK + GROW * ch:w * BANK + GROW * ch + GROW], row[:, P * ch:P * ch + P], ident[0:GROW, 0:GROW])
                last.then_inc(sem(f"columns_turned{layer}"), 1)

            def ends(layer, w):
                pe.wait_ge(sem(f"ends_spread{layer}"), w + 1)
                mm(PS[:, (2 + w) * BANK:(2 + w) * BANK + NT * GROW], ones[0:GROW, :], endx[:].rearrange("p a b -> p (a b)"),
                   start=True, stop=True).then_inc(sem(f"ends_out{layer}"), 1)

            def spread(b, row, d, j, masks=None):
                for lo, hi in segments(0):
                    last = mm(ps(b, lo, hi), sel(d, j), row[:, lo:hi], start=True, stop=masks is None)
                    if masks is not None:
                        n = (hi - lo) // P
                        last = mm(ps(b, lo, hi), ident_b, masks.unsqueeze(1).to_broadcast([P, n, P]), start=False, stop=True)
                return last

            def mlstm():
                pe.wait_ge(sem("ml_ready"), 1)
                for u in range(2 * HEADS):
                    d, h = divmod(u, HEADS)
                    r = 64 * (h % 2)
                    q, k = proj[r:r + 64, MLQ + h // 2, :], proj[r:r + 64, MLK + h // 2, :]
                    if u >= 1:
                        pe.wait_ge(sem("ml_den"), u)
                    spread(0, e_A, d, h, incl[d]).then_inc(sem("ml_pe"), 1)
                    if u >= 1:
                        pe.wait_ge(sem("ml_out"), u)
                    for ch in range(NT):
                        last = mm(ps(2, P * ch, P * ch + P), k[:, P * ch:P * ch + P], q[:, P * ch:P * ch + P], start=True, stop=True)
                    last.then_inc(sem("ml_pe"), 1)
                    spread(4, e_inter, d, h).then_inc(sem("ml_pe"), 1)
                    for i, ch in enumerate(ORDER[d][:5]):
                        pe.wait_ge(sem("ml_kw"), 6 * u + ch + 1)
                        b = 6 + i % 2
                        if i >= 2 or u >= 1:
                            pe.wait_ge(sem("ml_state"), 5 * u + max(i - 1, 0))
                        o = PS[r:r + 64, b * BANK:b * BANK + 128]
                        mm(o, kw[:, ch, :], tok_e[:, ch, 512 + P * h:512 + P * h + P], start=True, stop=True)
                        mm(PS[r:r + 64, b * BANK + 128:b * BANK + 256], kw[:, ch, :], ones, start=True, stop=True).then_inc(sem("ml_u"), 1)
                    pe.wait_ge(sem("ml_probs"), u + 1)
                    pe.wait_ge(sem("ml_qt"), u + 1)
                    pe.wait_ge(sem("ml_state"), 5 * u + 5)
                    for which in range(2):
                        for i, ch in enumerate(ORDER[d]):
                            at = P * ch
                            o = ps(2 - 2 * which, at, at + P)
                            if i > 0:
                                mm(o, cst[r:r + 64, ch, 128 * which:128 * which + 128], qt[r:r + 64, at:at + P], start=True, stop=False)
                            w = ones if which else tok_e[:, ch, 512 + P * h:512 + P * h + P]
                            last = mm(o, w, pm[:, at:at + P], start=i == 0, stop=True)
                        last.then_inc(sem("ml_pe"), 1)
                    spread(4, e_em, d, h).then_inc(sem("ml_pe"), 1)

            def deltanet():
                pe.wait_ge(sem("dn_cols"), 1)
                for u, (d, i, c) in enumerate(UNITS):
                    tc = slice(P * c, P * c + P)
                    lat = c >= 2
                    if u >= 1:
                        pe.wait_ge(sem("dn_state"), u)
                    for h in range(HEADS):
                        mm(ps(0, P * h, P * h + P), sel(d, h), o_gb[:, tc], start=True, stop=False)
                        mm(ps(0, P * h, P * h + P), ident_b, strict[d], start=False, stop=True)
                    for h in range(HEADS):
                        k = proj[:, DNK + h, tc]
                        last = mm(ps(1, P * h, P * h + P), k, k, start=True, stop=True)
                    last.then_inc(sem("dn_a_in"), 1)
                    if lat:
                        for h in range(HEADS):
                            mm(ps(2, P * h, P * h + P), sel(d, h), o_g[:, tc], start=True, stop=False)
                            mm(ps(2, P * h, P * h + P), ident_b, incl[d], start=False, stop=True)
                        for h in range(HEADS):
                            mm(ps(3, P * h, P * h + P), proj[:, DNK + h, tc], proj[:, DNQ + h, tc], start=True, stop=True)
                        for h in range(HEADS):
                            last = mm(ps(4, P * h, P * h + P), sel(d, h), o_eg[:, tc], start=True, stop=True)
                        last.then_inc(sem("dn_q_in"), 1)
                    pe.wait_ge(sem("dn_level"), LEVELS * u + 1)
                    for h in range(HEADS):
                        last = mm(ps(5, P * h, P * h + P), LV[0][:, P * h:P * h + P], ident, start=True, stop=True)
                    last.then_inc(sem("dn_y_in"), 1)
                    for k in range(1, LEVELS):
                        pe.wait_ge(sem("dn_level"), LEVELS * u + k + 1)
                        pe.wait_ge(sem("dn_x"), 2 * (LEVELS * u + k))
                        for h in range(HEADS):
                            last = mm(ps(5, P * h, P * h + P), LV[k][:, P * h:P * h + P], X[:, P * h:P * h + P], start=True, stop=True)
                        last.then_inc(sem("dn_y_in"), 1)
                        pe.wait_ge(sem("dn_y"), 6 * u + k)
                        for h in range(HEADS):
                            s = slice(P * h, P * h + P)
                            mm(ps(6, P * h, P * h + P), XT[:, s], Y[:, s], start=True, stop=True)
                        for h in range(HEADS):
                            s = slice(P * h, P * h + P)
                            last = mm(ps(7, P * h, P * h + P), Y[:, s], XT[:, s], start=True, stop=True)
                        last.then_inc(sem("dn_z_in"), 1)
                    pe.wait_ge(sem("dn_x"), 2 * LEVELS * (u + 1))
                    pe.wait_ge(sem("dn_scaled"), 3 * u + 3)
                    for h in range(HEADS):
                        s = slice(P * h, P * h + P)
                        last = mm(ps(5, P * h, P * h + P), KB[:, s], XT[:, s], start=True, stop=True)
                    last.then_inc(sem("dn_w_in"), 1)
                    if i > 0:
                        pe.wait_ge(sem("dn_w"), u + 1)
                    for h in range(HEADS):
                        s = slice(P * h, P * h + P)
                        last = mm(ps(6, P * h, P * h + P), XT[:, s], VB[:, s], start=True, stop=i == 0)
                        if i > 0:
                            last = mm(ps(6, P * h, P * h + P), WT[:, s], ST[:, s], start=False, stop=True)
                    last.then_inc(sem("dn_u_in"), 1)
                    pe.wait_ge(sem("dn_u"), u + 1)
                    if lat:
                        pe.wait_ge(sem("dn_q"), 2 * (4 * d + i - 2) + 2)
                        for h in range(HEADS):
                            s = slice(P * h, P * h + P)
                            mm(ps(7, P * h, P * h + P), ST[:, s], QG[:, s], start=True, stop=False)
                            last = mm(ps(7, P * h, P * h + P), U[:, s], ATTN[:, s], start=False, stop=True)
                        last.then_inc(sem("dn_o_in"), 1)
                    for h in range(HEADS):
                        s = slice(P * h, P * h + P)
                        last = mm(ps(0, P * h, P * h + P), KDC[:, s], U[:, s], start=True, stop=True)
                    last.then_inc(sem("dn_s_in"), 1)

            def up(layer, c0):
                stage = f"up{layer}"
                j0 = PLAN[stage][0]

                def body(k, i):
                    for half in range(2):
                        f = 2 * (k // 2) + half
                        which = k % 2
                        a = 4 * which + 2 * half
                        free = sem(f"ffn_act{layer}" if which else f"ffn_silu{layer}")
                        if isinstance(i, int):
                            if 4 * i + f >= 2:
                                pe.wait_ge(free, 4 * i + f - 1)
                        elif f >= 2:
                            pe.wait_ge(free, 4 * i + (f - 1))
                        for kk in range(KD):
                            for lo, hi in segments(c0):
                                last = mm(ps(a, lo - c0, hi - c0), wslot(j0 + k, kk, half), hT[:, kk, lo:hi],
                                          start=kk == 0, stop=kk == KD - 1)
                        last.then_inc(sem("products"), 1)

                n = PLAN[stage][1]
                for k in range(4):
                    arrived(j0 + k)
                    body(k, 0)
                with pe.Fori(1, n // 4) as i:
                    for k in range(4):
                        arrived(j0 + k, i)
                        if k // 2 == 0:
                            free = sem(f"ffn_act{layer}" if k % 2 else f"ffn_silu{layer}")
                            pe.wait_ge(free, 4 * i)
                        body(k, i)
                for k in range(n // 4 * 4, n):
                    arrived(j0 + k)
                    body(k % 4, n // 4)

            def down(layer, c0):
                stage = f"down{layer}"
                j0, n_loads, _, _ = PLAN[stage]

                def body(k, i):
                    n, half = k // 2, k % 2
                    a = 2 * n
                    if half == 0 and not (isinstance(i, int) and i == 0):
                        pe.wait_ge(sem(f"down_added{layer}"), per * (2 * i + n - 1))
                    for kk in range(11):
                        for lo, hi in segments(c0):
                            last = mm(ps(a, lo - c0, hi - c0), ring[:, (j0 + k) % SLOTS, 128 * kk:128 * kk + 128],
                                      proj[:, 11 * half + kk, lo:hi], start=half == 0 and kk == 0, stop=half == 1 and kk == 10)
                    last.then_inc(sem("products"), 1)

                per = 2 if c0 == 0 else 1
                pe.wait_ge(sem(f"ffn_act{layer}"), FC)
                for k in range(4):
                    arrived(j0 + k)
                    body(k, 0)
                with pe.Fori(1, n_loads // 4) as i:
                    for k in range(4):
                        arrived(j0 + k, i)
                        body(k, i)

            for layer in range(2):
                tag = f"mix{layer}"
                if layer == 0:
                    pe.wait_ge(sem("x_moved"), 8)
                norm_sums(tag, 0)
                pe.wait_ge(sem(f"h_ready_{tag}"), 2 * KD)
                project(f"proj{layer}", 0, hT, f"proj_moved{layer}")
                pe.wait_ge(sem(f"proj_moved{layer}"), 24 if layer == 0 else 22)
                if layer == 0:
                    turn("even", None)
                    pe.wait_ge(sem("moved_even"), 3 * NT)
                    gates(0)
                    pe.wait_ge(sem("gates_moved0"), 2)
                    rope(0)
                    pe.wait_ge(sem("rope_done0"), 8)
                    attention(0)
                    pe.wait_ge(sem("att_y0"), 24)
                    pe.wait_ge(sem("mod_ready"), 2)
                    head_norm_sums("da")
                    pe.wait_ge(sem("hms_da"), HEADS)
                    row_columns(0, [e_ib])
                    ends(0, 0)
                    ends(0, 1)
                    mlstm()
                    pe.wait_ge(sem("ml_out"), 2 * HEADS)
                    head_norm_sums("ml")
                    pe.wait_ge(sem("y_gated0"), HEADS)
                else:
                    pe.wait_ge(sem("conv_silu"), 12)
                    head_norm_sums("l2")
                    pe.wait_ge(sem("hnorm_l2"), 8)
                    turn("odd", None)
                    pe.wait_ge(sem("moved_odd"), 3 * NT)
                    gates(1)
                    head_norm_sums("qk")
                    pe.wait_ge(sem("hnorm_qk"), 5)
                    pe.wait_ge(sem("gates_moved1"), 2)
                    rope(1)
                    pe.wait_ge(sem("keys_spread"), 64)
                    attention(1)
                    pe.wait_ge(sem("att_y1"), 32)
                    row_columns(1, [o_g, o_gb])
                    ends(1, 0)
                    deltanet()
                    pe.wait_ge(sem("dn_state"), len(UNITS))
                    pe.wait_ge(sem("dn_o"), 8)
                    head_norm_sums("dn")
                    pe.wait_ge(sem("y_gated1"), HEADS)
                c0 = 0 if layer == 0 else CTX
                project(f"out{layer}", c0, hT, f"out_added{layer}", 2 if layer == 0 else 1)
                pe.wait_ge(sem(f"out_added{layer}"), 8 * (2 if c0 == 0 else 1))
                norm_sums(f"ffn{layer}", c0)
                pe.wait_ge(sem(f"h_ready_ffn{layer}"), KD * (2 if c0 == 0 else 1))
                up(layer, c0)
                down(layer, c0)
                pe.wait_ge(sem(f"down_added{layer}"), 8 * (2 if c0 == 0 else 1))
            norm_sums("final", CTX)
            for i in range(8):
                t, half = divmod(i, 2)
                pe.wait_ge(sem("final_normed"), 8)
                if i >= 2:
                    pe.wait_ge(sem("out_moved"), i - 1)
                for k in range(4):
                    last = tr(ps(2 + i % 2, P * k, P * k + P), hT[:, 4 * half + k, CTX + P * t:CTX + P * t + P], ident)
                last.then_inc(sem("out_turned"), 1)

        @block.scalar
        def _(act):
            step_no = [0]

            def A(out_, in_, f, **kw):
                return nc.scalar.activation(out_, in_, f, **kw)

            def then(ins):
                step_no[0] += 1
                ins.then_inc(sem("act_step"), 1)
                act.wait_ge(sem("act_step"), step_no[0])

            act.wait_ge(sem("vec_moved"), 2)
            A(silu_c[:].rearrange("p k s -> p s k"), vec_b[:, V_C:V_C + 16].rearrange("p (s k) -> p s k", s=2), ACT.Silu).then_inc(sem("silu_c"), 1)
            for k in range(0, KD):
                act.wait_ge(sem("x_turned"), k + 1)
                A(xT[:, k, :], ps(2 + 2 * (k % 2), 0, T), ACT.Copy).then_inc(sem("x_moved"), 1)
            act.wait_ge(sem("lam_sums"), 1)
            A(small[:, 2:4], small[:, 0:2], ACT.Exp).then_inc(sem("lam_exp"), 1)
            act.wait_ge(sem("gates_in"), 16 * 11)
            act.wait_ge(sem("vec_moved"), 2)
            A(gate_b[:, 4:5], gate_b[:, 3:4], ACT.Exp).then_inc(sem("lam_exp"), 1)
            A(small[:, 4:5], vec_b[:, G_DA:G_DA + 1], ACT.Copy, scale=1.0 - LAM_INIT).then_inc(sem("lam_exp"), 1)

            norm_no = [0]

            def norm(tag, c0, shift):
                n = norm_no[0]
                for k in range(KD):
                    if n or k >= 2:
                        act.wait_ge(sem("squares_summed"), max(n * KD + k - 1, n * KD))
                    if k == 0:
                        act.wait_ge(sem("x_moved"), 8)
                    A(sq[:, k % 2, c0:T], xT[:, k, c0:T], ACT.Square).then_inc(sem("squared"), 1)
                act.wait_ge(sem("mean_square"), n + 1)
                A(rs[:, 0, c0:T], rs[:, 1, c0:T], ACT.Sqrt).then_inc(sem("root"), 1)
                norm_no[0] += 1
                if shift is None:
                    return
                layer, at = shift
                parts = [(CTX, T, 0)] + ([(0, CTX, 1)] if c0 == 0 else [])
                m = 0
                for k in range(KD):
                    for lo, hi, s in parts:
                        m += 1
                        act.wait_ge(sem(f"h_scaled_{tag}"), m)
                        A(hT[:, k, lo:hi], hT[:, k, lo:hi], ACT.Identity, bias=modT[:, layer, at + k, s:s + 1]).then_inc(sem(f"h_ready_{tag}"), 1)

            def move(stage):
                for i, (srcs, dst) in enumerate(transposes(stage)):
                    act.wait_ge(sem(f"turned_{stage}"), i + 1)
                    A(dst, ps(i % 4, 0, P * len(srcs)), ACT.Copy).then_inc(sem(f"moved_{stage}"), 1)

            def head_norm(stage):
                items = head_norm_items(stage)
                for i in range(len(items) + 1):
                    if i < len(items):
                        src, _, _, _, _, n = items[i]
                        if i >= 2:
                            act.wait_ge(sem(f"hsum_{stage}"), i - 1)
                        A(sq[:, i % 2, 0:n], src, ACT.Square).then_inc(sem(f"hsq_{stage}"), 1)
                    if i >= 1:
                        n = items[i - 1][5]
                        act.wait_ge(sem(f"hms_{stage}"), i)
                        A(rs[:, (i - 1) % 2, 0:n], rs[:, (i - 1) % 2, 0:n], ACT.Sqrt).then_inc(sem(f"hroot_{stage}"), 1)

            def attention(layer):
                a = Att(layer)
                n = len(a.tiles)

                def exps(i):
                    for m in range(a.maps):
                        g = i * a.maps + m
                        act.wait_ge(sem(f"att_max{layer}"), g + 1)
                        if i >= 2:
                            act.wait_ge(sem(f"att_turned{layer}"), i - 1)
                        nk = a.keys(i)
                        b = 2 * m if a.maps == 2 else 2 * (i % 2)
                        o = 8 * (i % 2)
                        A(a.E[i % 2][m][:, 0:nk], ps(b, 0, nk), ACT.Exp, bias=small[:, 8 + o + m:9 + o + m], scale=64 ** -0.5,
                          accum_out=small[:, 10 + o + m:11 + o + m]).then_inc(sem(f"att_exp{layer}"), 1)

                exps(0)
                for i in range(n):
                    if i + 1 < n:
                        exps(i + 1)
                    act.wait_ge(sem(f"att_turned{layer}"), i + 1)
                    if i >= 2:
                        act.wait_ge(sem(f"att_out{layer}"), i - 1)
                    nk = a.keys(i)
                    A(a.PT[i % 2][:, 0:nk], ps(4, 0, nk), ACT.Copy).then_inc(sem(f"att_pt{layer}"), 1)

            def soft_rows(layer):
                if layer == 0:
                    act.wait_ge(sem("rows_in0"), 1)
                    then(A(e_t, rowF, ACT.Abs))
                    then(A(e_t, e_t, ACT.Exp, scale=-1.0))
                    A(e_t, e_t, ACT.Ln, bias=1.0).then_inc(sem("soft0"), 1)
                    act.wait_ge(sem("rows_diff0"), 1)
                    A(e_inter, e_inter, ACT.Exp)
                    A(e_em, e_m, ACT.Exp, scale=-1.0)
                    A(endr[:, 4, 0:NT], endr[:, 4, 0:NT], ACT.Exp).then_inc(sem("rows_exp0"), 1)
                else:
                    act.wait_ge(sem("rows_in1"), 1)
                    for k, row in enumerate((o_rowI, o_rowF)):
                        dst = (o_gb, o_t)[k]
                        then(A(dst, row, ACT.Abs))
                        then(A(dst, dst, ACT.Exp, scale=-1.0))
                        A(dst, dst, ACT.Ln, bias=1.0).then_inc(sem("soft1"), 1)
                    act.wait_ge(sem("rows_diff1"), 1)
                    A(o_eg, o_g, ACT.Exp).then_inc(sem("rows_exp1"), 1)

            def mlstm():
                act.wait_ge(sem("ml_wexp"), 2)
                A(cols[:, 1], cols[:, 1], ACT.Exp).then_inc(sem("ml_ready"), 1)
                act.wait_ge(sem("ml_ready"), 1)
                for u in range(2 * HEADS):
                    d, h = divmod(u, HEADS)
                    r = u
                    if u >= 1:
                        act.wait_ge(sem("ml_u"), 5 * u)
                    for ch in range(NT):
                        A(kw[:, ch, :], tok_e[:, ch, 1024 + 64 * h:1088 + 64 * h], ACT.Copy, scale=cols[:, 1, ch, r:r + 1]).then_inc(sem("ml_kw"), 1)
                    act.wait_ge(sem("ml_pe"), 6 * u + 1)
                    for ch in range(NT):
                        last = A(pexp[:, P * ch:P * ch + P], ps(0, P * ch, P * ch + P), ACT.Exp, bias=cols[:, 0, ch, r:r + 1])
                    last.then_inc(sem("ml_exp"), 1)
                    act.wait_ge(sem("ml_pe"), 6 * u + 5)
                    if u >= 1:
                        act.wait_ge(sem("ml_out"), u)
                    A(den, ps(0, 0, T), ACT.Abs).then_inc(sem("ml_den"), 1)

            def deltanet():
                act.wait_ge(sem("dn_wexp"), 2)
                A(cols[:, 0:3], cols[:, 0:3], ACT.Exp)
                A(endb[:], endb[:], ACT.Exp).then_inc(sem("dn_cols"), 1)
                for u, (d, i, c) in enumerate(UNITS):
                    r = 4 * d
                    act.wait_ge(sem("dn_a_in"), u + 1)
                    if u == 0:
                        act.wait_ge(sem("dn_cols"), 1)
                    for h in range(HEADS):
                        last = A(X[:, P * h:P * h + P], ps(0, P * h, P * h + P), ACT.Exp, bias=cols[:, 3, c, r + h:r + h + 1])
                    last.then_inc(sem("dn_aexp"), 1)
                    if c >= 2:
                        act.wait_ge(sem("dn_q_in"), 4 * d + i - 1)
                        for h in range(HEADS):
                            last = A(Y[:, P * h:P * h + P], ps(2, P * h, P * h + P), ACT.Exp, bias=cols[:, 3, c, r + h:r + h + 1])
                        last.then_inc(sem("dn_qexp"), 1)
                        act.wait_ge(sem("dn_q"), 2 * (4 * d + i - 2) + 1)
                    for k in range(1, LEVELS):
                        act.wait_ge(sem("dn_y_in"), LEVELS * u + k + 1)
                        if k >= 2:
                            act.wait_ge(sem("dn_z_in"), 6 * u + k - 1)
                        A(Y, ps(5, 0, 512), ACT.Copy).then_inc(sem("dn_y"), 1)
                    act.wait_ge(sem("dn_w_in"), u + 1)
                    A(WT, ps(5, 0, 512), ACT.Copy, scale=-1.0).then_inc(sem("dn_w"), 1)

            def gate_values(layer, first, c0, stage):
                for h in range(HEADS):
                    A(proj[:, first + h, c0:T], proj[:, first + h, c0:T], ACT.Sigmoid if layer == 0 else ACT.Silu).then_inc(sem(f"out_gate{layer}"), 1)

            def up(layer, c0):
                _, _, _, done = PLAN[f"up{layer}"]
                w = T - c0

                def body(f, i):
                    act.wait_ge(sem("products"), 8 * i + (done + 4 * (f // 2) + f % 2 + 1))
                    if isinstance(i, int):
                        if 4 * i + f >= 2:
                            act.wait_ge(sem(f"ffn_act{layer}"), 4 * i + f - 1)
                    elif f >= 1:
                        act.wait_ge(sem(f"ffn_act{layer}"), 4 * i + (f - 1))
                    A(sq[:, f % 2, 0:w], ps(2 * (f % 2), 0, w), ACT.Silu).then_inc(sem(f"ffn_silu{layer}"), 1)

                for f in range(4):
                    body(f, 0)
                with act.Fori(1, FC // 4) as i:
                    act.wait_ge(sem(f"ffn_act{layer}"), 4 * i - 1)
                    for f in range(4):
                        body(f, i)
                for f in range(FC % 4):
                    body(f, FC // 4)

            for layer in range(2):
                c0 = 0 if layer == 0 else CTX
                act.wait_ge(sem("mod_ready"), layer + 1)
                norm(f"mix{layer}", 0, (layer, SH1))
                if layer == 0:
                    move("even")
                    attention(0)
                    head_norm("da")
                    soft_rows(0)
                    mlstm()
                    gate_values(0, MLO, 0, "ml")
                    act.wait_ge(sem("ml_out"), 2 * HEADS)
                    head_norm("ml")
                else:
                    for b in range(12):
                        act.wait_ge(sem("conv_sum"), b + 1)
                        A(proj[:, DNQ + b, :], rs[:, b % 2, :], ACT.Silu).then_inc(sem("conv_silu"), 1)
                    gate_values(1, DNZ, CTX, "dn")
                    act.wait_ge(sem("conv_silu"), 12)
                    head_norm("l2")
                    move("odd")
                    head_norm("qk")
                    attention(1)
                    soft_rows(1)
                    deltanet()
                    act.wait_ge(sem("dn_o"), 8)
                    head_norm("dn")
                act.wait_ge(sem(f"out_added{layer}"), 8 * (2 if c0 == 0 else 1))
                norm(f"ffn{layer}", c0, (layer, SH2))
                up(layer, c0)
                act.wait_ge(sem(f"down_added{layer}"), 8 * (2 if c0 == 0 else 1))
            norm("final", CTX, None)
            for i in range(8):
                t, half = divmod(i, 2)
                act.wait_ge(sem("out_turned"), i + 1)
                A(out_tok[:, t, 512 * half:512 * half + 512], ps(2 + i % 2, 0, 512), ACT.Copy).then_inc(sem("out_moved"), 1)

        @block.vector
        def _(dve):
            V = nc.vector
            step_no = [0]

            def then(ins):
                step_no[0] += 1
                ins.then_inc(sem("dve_step"), 1)
                dve.wait_ge(sem("dve_step"), step_no[0])

            dve.wait_ge(sem("vec_turned"), 2)
            V.tensor_copy(vec_a[:], ps(0, 0, 96)).then_inc(sem("vec_moved"), 1)
            V.tensor_copy(vec_b[:], ps(1, 0, NVEC)).then_inc(sem("vec_moved"), 1)
            dve.wait_ge(sem("gates_in"), 16 * 11)
            lam2 = lam_in.rearrange("p (a b) n -> p a b n", b=2)
            then(V.tensor_tensor(lam_tmp, lam2[:, :, 0, :], lam2[:, :, 1, :], ALU.mult))
            V.tensor_reduce(small[:, 0:2], lam_tmp, AX_X, ALU.add).then_inc(sem("lam_sums"), 1)
            dve.wait_ge(sem("lam_exp"), 2)
            then(V.tensor_tensor(small[:, 5:6], small[:, 3:4], small[:, 2:3], ALU.subtract))
            then(V.tensor_scalar(small[:, 6:7], small[:, 5:6], LAM_INIT, None, ALU.subtract))
            then(V.tensor_scalar(gate_b[:, 5:6], gate_b[:, 4:5], -1.0, None, ALU.mult))
            dve.wait_ge(sem("vec_moved"), 2)
            mod_flat = modT[:].rearrange("p l n s -> p (l n) s")

            def modulation(lo, hi, scales):
                then(V.tensor_tensor(mod_flat[:, lo:hi], PS[:, 6 * BANK + 2 * lo:6 * BANK + 2 * hi].rearrange("p (n s) -> p n s", s=2),
                                     vec_a[:, lo:hi].unsqueeze(2).to_broadcast([P, hi - lo, 2]), ALU.add))
                for l, j in scales:
                    at = (SC1, SC2)[j]
                    g = vec_b[:, (G_MIX, G_FFN)[j] + 8 * l:(G_MIX, G_FFN)[j] + 8 * l + 8]
                    last = V.scalar_tensor_tensor(out=gmT[:, l, j], in0=modT[:, l, at:at + 8, :], scalar=1.0,
                                                  in1=g.unsqueeze(2).to_broadcast([P, KD, 2]), op0=ALU.add, op1=ALU.mult)
                last.then_inc(sem("mod_ready"), 1)

            dve.wait_ge(sem("products"), 16)
            modulation(0, 16, [(0, 0)])

            norm_no = [0]

            def norm(tag, c0, gains, last_gain=None):
                n = norm_no[0]
                dve.wait_ge(sem("squares_summed"), KD * (n + 1))
                V.tensor_scalar(rs[:, 1, c0:T], PS[:, 0:T - c0], 1.0 / D, EPS, ALU.mult, ALU.add).then_inc(sem("mean_square"), 1)
                dve.wait_ge(sem("root"), n + 1)
                then(V.reciprocal(rs[:, 1, c0:T], rs[:, 0, c0:T]))
                norm_no[0] += 1
                parts = [(CTX, T, 0)] + ([(0, CTX, 1)] if c0 == 0 else [])
                for k in range(KD):
                    for lo, hi, s in parts:
                        g = gains[:, k, s:s + 1] if gains is not None else last_gain[:, k:k + 1]
                        V.scalar_tensor_tensor(out=hT[:, k, lo:hi], in0=xT[:, k, lo:hi], scalar=g, in1=rs[:, 1, lo:hi],
                                               op0=ALU.mult, op1=ALU.mult).then_inc(sem(f"h_scaled_{tag}" if gains is not None else "final_normed"), 1)

            def project_out(layer):
                n = 24 if layer == 0 else 22
                _, _, _, done = PLAN[f"proj{layer}"]
                with dve.Fori(0, n // 8) as i:
                    for b in range(8):
                        dve.wait_ge(sem("products"), 8 * i + (done + b + 1))
                        V.tensor_scalar(proj[:, bass.ds(8 * i + b, 1), :].rearrange("p a t -> p (a t)"), ps(2 * (b % 4), 0, T), 1.0, None,
                                        ALU.mult).then_inc(sem(f"proj_moved{layer}"), 1)
                for b in range(n // 8 * 8, n):
                    dve.wait_ge(sem("products"), done + b + 1)
                    V.tensor_scalar(proj[:, b, :], ps(2 * (b % 4), 0, T), 1.0, None, ALU.mult).then_inc(sem(f"proj_moved{layer}"), 1)

            def add_in(k, b, layer, ga, c0, signal):
                parts = [(CTX, T, 0)] + ([(0, CTX, 1)] if c0 == 0 else [])
                for lo, hi, s in parts:
                    xs = xT[:, bass.ds(k, 1), lo:hi].rearrange("p a t -> p (a t)")
                    g = modT[:, layer, bass.ds(ga + k, 1), s:s + 1].rearrange("p a t -> p (a t)")
                    V.scalar_tensor_tensor(out=xs, in0=ps(b, lo - c0, hi - c0), scalar=g, in1=xs, op0=ALU.mult, op1=ALU.add).then_inc(sem(signal), 1)

            def head_norm(stage, gate=None):
                items = head_norm_items(stage)
                for i in range(len(items) + 1):
                    if i < len(items):
                        _, _, scale, _, _, n = items[i]
                        dve.wait_ge(sem(f"hsum_{stage}"), i + 1)
                        if i >= 2:
                            dve.wait_ge(sem(f"hnorm_{stage}"), i - 1)
                        V.tensor_scalar(rs[:, i % 2, 0:n], ps(2 * (i % 2), 0, n), scale, EPS, ALU.mult, ALU.add).then_inc(sem(f"hms_{stage}"), 1)
                    if i >= 1:
                        src, _, _, gain, dst, n = items[i - 1]
                        r = rs[:, (i - 1) % 2, 0:n]
                        dve.wait_ge(sem(f"hroot_{stage}"), i)
                        then(V.reciprocal(r, r))
                        V.scalar_tensor_tensor(out=dst, in0=src, scalar=gain, in1=r, op0=ALU.mult, op1=ALU.mult).then_inc(sem(f"hnorm_{stage}"), 1)

            def rope(layer):
                t1, t2 = rs[:, 0, 0:LAT], rs[:, 1, 0:LAT]
                cos, sin = rot_at[layer][:, 0:LAT], rot_at[layer][:, LAT:2 * LAT]
                dve.wait_ge(sem("rotary_in"), 16 * (layer + 1))
                for i, b in enumerate(ROPE[layer]):
                    xs = proj[:, b, CTX:T]
                    dve.wait_ge(sem(f"rope_swapped{layer}"), i + 1)
                    if i >= 1:
                        dve.wait_ge(sem(f"rope_done{layer}"), i)
                    V.tensor_tensor(t1, xs, cos, ALU.mult).then_inc(sem("rope_parts"), 1)
                    V.tensor_tensor(t2, ps(4 + i % 2, 0, LAT), sin, ALU.mult).then_inc(sem("rope_parts"), 1)
                    rope_no[0] += 2
                    dve.wait_ge(sem("rope_parts"), rope_no[0])
                    V.tensor_tensor(xs, t1, t2, ALU.add).then_inc(sem(f"rope_done{layer}"), 1)

            rope_no = [0]

            def gate_rows(layer):
                rows = (rowI, rowF) if layer == 0 else (o_rowI, o_rowF)
                for kind in range(2):
                    dve.wait_ge(sem("gate_rows"), 2 * layer + kind + 1)
                    src = PS[0:GROW, (4 + 2 * kind) * BANK:(4 + 2 * kind) * BANK + T]
                    if layer == 0:
                        ins = V.tensor_scalar(rows[kind], src, gate_b[:, kind:kind + 1], None, ALU.add)
                    elif kind == 0:
                        ins = V.tensor_copy(rows[kind], src)
                    else:
                        ins = V.tensor_scalar(rows[kind], src, gate_b[:, 2:3], None, ALU.add)
                    ins.then_inc(sem(f"gates_moved{layer}"), 1)

            def attention(layer):
                a = Att(layer)
                n = len(a.tiles)

                def maxima(i):
                    o = 8 * (i % 2)
                    for m in range(a.maps):
                        g = i * a.maps + m
                        b = 2 * m if a.maps == 2 else 2 * (i % 2)
                        dve.wait_ge(sem(f"att_scores{layer}"), g + 1)
                        then(V.tensor_reduce(small[:, 12 + o + m:13 + o + m], ps(b, 0, a.keys(i)), AX_X, ALU.max))
                        V.tensor_scalar(small[:, 8 + o + m:9 + o + m], small[:, 12 + o + m:13 + o + m], -(64 ** -0.5), None,
                                        ALU.mult).then_inc(sem(f"att_max{layer}"), 1)

                maxima(0)
                for i in range(n):
                    o = 8 * (i % 2)
                    nk = a.keys(i)
                    e = [a.E[i % 2][m][:, 0:nk] for m in range(a.maps)]
                    dve.wait_ge(sem(f"att_exp{layer}"), a.maps * (i + 1))
                    then(V.reciprocal(small[:, 12 + o:12 + o + a.maps], small[:, 10 + o:10 + o + a.maps]))
                    if a.maps == 2:
                        then(V.tensor_tensor(small[:, 14 + o:15 + o], small[:, 13 + o:14 + o], small[:, 6:7], ALU.mult))
                        then(V.tensor_scalar(e[0], e[0], small[:, 12 + o:13 + o], None, ALU.mult))
                        V.scalar_tensor_tensor(out=e[0], in0=e[1], scalar=small[:, 14 + o:15 + o], in1=e[0], op0=ALU.mult,
                                               op1=ALU.add).then_inc(sem(f"att_probs{layer}"), 1)
                    else:
                        V.tensor_scalar(e[0], e[0], small[:, 12 + o:13 + o], None, ALU.mult).then_inc(sem(f"att_probs{layer}"), 1)
                    if i + 1 < n:
                        maxima(i + 1)
                    if i >= 1:
                        output(i - 1)
                output(n - 1)

            def att_output(layer):
                a = Att(layer)

                def go(i):
                    dve.wait_ge(sem(f"att_out{layer}"), i + 1)
                    lo, hi = a.rows(i)
                    V.tensor_copy(a.y(i), PS[lo:hi, 7 * BANK:7 * BANK + P]).then_inc(sem(f"att_y{layer}"), 1)
                return go

            def ends_of(row, dst, d_rows=(0, 1)):
                v = row.rearrange("p (c n) -> p c n", n=P)
                then(V.tensor_copy(dst[0:32, 0:NT], v[0:32, :, P - 1]))
                then(V.tensor_copy(dst[32:GROW, 0:NT], v[32:GROW, :, 0]))

            def spread_ends(layer, w, row):
                if w:
                    dve.wait_ge(sem(f"ends_out{layer}"), w)
                V.tensor_tensor(endx[:], ident[0:GROW, 0:GROW].unsqueeze(1).to_broadcast([GROW, NT, GROW]),
                                row.unsqueeze(2).to_broadcast([GROW, NT, GROW]), ALU.mult).then_inc(sem(f"ends_spread{layer}"), 1)

            def turned(b, s):
                return PS[:, b * BANK:b * BANK + NT * GROW].rearrange("p (c r) -> p c r", c=NT)[:, :, s]

            def bykey(f):
                for d in range(2):
                    f(slice(4 * d, 4 * d + 4), slice(32 * d, 32 * d + 4))

            def rows_even():
                dve.wait_ge(sem("gates_moved0"), 2)
                dve.wait_ge(sem("att_y0"), 24)
                dve.wait_ge(sem("att_out0"), 24)
                V.memset(small[:, 7:8], 0.0).then_inc(sem("rows_in0"), 1)
                dve.wait_ge(sem("soft0"), 1)
                then(V.scalar_tensor_tensor(out=e_logf, in0=rowF, scalar=0.0, in1=e_t, op0=ALU.min, op1=ALU.subtract))
                then(V.tensor_tensor_scan(e_m[0:32], e_logf[0:32], rowI[0:32], 0.0, ALU.add, ALU.max))
                r = slice(32, GROW)
                then(V.tensor_tensor_scan(e_m[r, 0:CTX][:, ::-1], e_logf[r, 0:CTX][:, ::-1], rowI[r, 0:CTX][:, ::-1], 0.0, ALU.add, ALU.max))
                then(V.tensor_tensor_scan(e_m[r, CTX:T][:, ::-1], e_logf[r, CTX:T][:, ::-1], rowI[r, CTX:T][:, ::-1], e_m[r, 0:1], ALU.add, ALU.max))
                then(V.tensor_copy(e_t.rearrange("p (c n) -> p c n", n=P), resets))
                then(V.tensor_tensor_scan(e_b[0:32], e_t[0:32], e_logf[0:32], 0.0, ALU.mult, ALU.add))
                then(V.tensor_tensor_scan(e_b[r][:, ::-1], e_t[r][:, ::-1], e_logf[r][:, ::-1], 0.0, ALU.mult, ALU.add))
                ends_of(e_m, endr[:, 0])
                ends_of(e_b, endr[:, 1])
                then(V.memset(endr[:, 2, :], 0.0))
                then(V.tensor_copy(endr[0:32, 2, 1:NT], endr[0:32, 0, 0:NT - 1]))
                then(V.tensor_copy(endr[r, 2, 0:1], endr[r, 0, 1:2]))
                then(V.tensor_copy(endr[r, 2, NT - 1:NT], endr[r, 0, 0:1]))
                then(V.tensor_copy(endr[r, 2, 2:NT - 1], endr[r, 0, 3:NT]))
                then(V.tensor_tensor(e_ib, rowI, e_b, ALU.subtract))
                then(V.tensor_tensor(e_A, e_b, e_m, ALU.subtract))
                m0 = endr[:, 2, 0:NT].unsqueeze(2).to_broadcast([GROW, NT, P])
                then(V.tensor_tensor(e_inter.rearrange("p (c n) -> p c n", n=P), e_A.rearrange("p (c n) -> p c n", n=P), m0, ALU.add))
                then(V.tensor_tensor(endr[:, 3, 0:NT], endr[:, 1, 0:NT], endr[:, 0, 0:NT], ALU.subtract))
                V.tensor_tensor(endr[:, 4, 0:NT], endr[:, 3, 0:NT], endr[:, 2, 0:NT], ALU.add).then_inc(sem("rows_diff0"), 1)
                dve.wait_ge(sem("rows_exp0"), 1)
                V.memset(small[:, 7:8], 0.0).then_inc(sem("rows_ready0"), 1)
                spread_ends(0, 0, endr[:, 3, 0:NT])
                spread_ends(0, 1, endr[:, 4, 0:NT])
                dve.wait_ge(sem("columns_turned0"), 1)
                bykey(lambda d, s: then(V.tensor_copy(cols[:, 0, :, d], turned(0, s))))
                dve.wait_ge(sem("ends_out0"), 2)
                bykey(lambda d, s: then(V.tensor_copy(endb[:, :, d], turned(3, s))))
                bykey(lambda d, s: V.tensor_tensor(cols[:, 1, :, d], cols[:, 0, :, d], turned(2, s), ALU.add).then_inc(sem("ml_wexp"), 1))
                dve.wait_ge(sem("ml_ready"), 1)

            def mlstm():
                for u in range(2 * HEADS):
                    d, h = divmod(u, HEADS)
                    r = 64 * (h % 2)
                    dve.wait_ge(sem("ml_pe"), 6 * u + 3)
                    dve.wait_ge(sem("ml_exp"), u + 1)
                    V.scalar_tensor_tensor(out=pm, in0=pexp, scalar=64 ** -0.5, in1=ps(2, 0, T), op0=ALU.mult, op1=ALU.mult).then_inc(sem("ml_probs"), 1)
                    V.scalar_tensor_tensor(out=qt[r:r + 64, :], in0=proj[r:r + 64, MLQ + h // 2, :], scalar=64 ** -0.5,
                                           in1=PS[r:r + 64, 4 * BANK:4 * BANK + T], op0=ALU.mult, op1=ALU.mult).then_inc(sem("ml_qt"), 1)
                    for i in range(5):
                        ch, nxt = ORDER[d][i], ORDER[d][i + 1]
                        dve.wait_ge(sem("ml_u"), 5 * u + i + 1)
                        src = PS[r:r + 64, (6 + i % 2) * BANK:(6 + i % 2) * BANK + 256]
                        if i == 0:
                            V.tensor_copy(cst[r:r + 64, nxt, :], src).then_inc(sem("ml_state"), 1)
                        else:
                            dve.wait_ge(sem("ml_state"), 5 * u + i)
                            V.scalar_tensor_tensor(out=cst[r:r + 64, nxt, :], in0=cst[r:r + 64, ch, :], scalar=endb[r:r + 64, ch, u:u + 1],
                                                   in1=src, op0=ALU.mult, op1=ALU.add).then_inc(sem("ml_state"), 1)
                    dve.wait_ge(sem("ml_den"), u + 1)
                    dve.wait_ge(sem("ml_pe"), 6 * u + 6)
                    then(V.tensor_tensor(den, den, ps(4, 0, T), ALU.max))
                    then(V.reciprocal(den, den))
                    y = hT[:, 4 + h, :]
                    if d == 0:
                        V.tensor_tensor(y, den, ps(2, 0, T), ALU.mult).then_inc(sem("ml_out"), 1)
                    else:
                        then(V.tensor_tensor(den, den, ps(2, 0, T), ALU.mult))
                        V.tensor_tensor(y, y, den, ALU.add).then_inc(sem("ml_out"), 1)

            def conv():
                n = 0
                for b in range(12):
                    acc = rs[:, b % 2, :]
                    src = proj[:, DNQ + b, :]
                    w = [vec_b[:, CONV + 12 * tap + b:CONV + 12 * tap + b + 1] for tap in range(3)]
                    if b >= 2:
                        dve.wait_ge(sem("conv_silu"), b - 1)
                    then(V.tensor_scalar(acc, src, w[1], None, ALU.mult))
                    for lo, hi in ((0, CTX), (CTX, T)):
                        then(V.scalar_tensor_tensor(out=acc[:, lo + 1:hi], in0=src[:, lo:hi - 1], scalar=w[0], in1=acc[:, lo + 1:hi],
                                                    op0=ALU.mult, op1=ALU.add))
                    for lo, hi in ((0, CTX), (CTX, T)):
                        ins = V.scalar_tensor_tensor(out=acc[:, lo:hi - 1], in0=src[:, lo + 1:hi], scalar=w[2], in1=acc[:, lo:hi - 1],
                                                     op0=ALU.mult, op1=ALU.add)
                        if lo == 0:
                            then(ins)
                    ins.then_inc(sem("conv_sum"), 1)

            def rows_odd():
                dve.wait_ge(sem("gates_moved1"), 2)
                dve.wait_ge(sem("att_y1"), 32)
                V.memset(small[:, 7:8], 0.0).then_inc(sem("rows_in1"), 1)
                dve.wait_ge(sem("soft1"), 2)
                r = slice(32, GROW)
                then(V.scalar_tensor_tensor(out=o_gb, in0=o_rowI, scalar=0.0, in1=o_gb, op0=ALU.min, op1=ALU.subtract))
                then(V.scalar_tensor_tensor(out=o_t, in0=o_rowF, scalar=0.0, in1=o_t, op0=ALU.max, op1=ALU.add))
                then(V.tensor_scalar(o_t, o_t, gate_b[:, 5:6], None, ALU.mult))
                then(V.tensor_copy(o_rst.rearrange("p (c n) -> p c n", n=P), resets))
                then(V.tensor_tensor_scan(o_g[0:32], o_rst[0:32], o_t[0:32], 0.0, ALU.mult, ALU.add))
                then(V.tensor_tensor_scan(o_g[r][:, ::-1], o_rst[r][:, ::-1], o_t[r][:, ::-1], 0.0, ALU.mult, ALU.add))
                then(V.tensor_tensor(o_gb, o_gb, o_g, ALU.add))
                ends_of(o_g, endr[:, 0])
                V.memset(small[:, 7:8], 0.0).then_inc(sem("rows_diff1"), 1)
                dve.wait_ge(sem("rows_exp1"), 1)
                V.memset(small[:, 7:8], 0.0).then_inc(sem("rows_ready1"), 1)
                spread_ends(1, 0, endr[:, 0, 0:NT])
                dve.wait_ge(sem("columns_turned1"), 1)
                bykey(lambda d, s: then(V.tensor_scalar(cols[:, 3, :, d], turned(0, s), -1.0, None, ALU.mult)))
                bykey(lambda d, s: then(V.tensor_copy(cols[:, 1, :, d], turned(1, s))))
                then(V.tensor_tensor(cols[:, 0], cols[:, 3], cols[:, 1], ALU.add))
                dve.wait_ge(sem("ends_out1"), 1)
                bykey(lambda d, s: then(V.tensor_copy(endb[:, :, d], turned(2, s))))
                bykey(lambda d, s: V.tensor_tensor(cols[:, 2, :, d], cols[:, 3, :, d], turned(2, s), ALU.add).then_inc(sem("dn_wexp"), 1))

            def deltanet():
                dve.wait_ge(sem("dn_cols"), 1)
                for u, (d, i, c) in enumerate(UNITS):
                    tc = slice(P * c, P * c + P)
                    lat = c >= 2
                    dve.wait_ge(sem("dn_aexp"), u + 1)
                    V.tensor_tensor(AT, X, ps(1, 0, 512), ALU.mult).then_inc(sem("dn_at"), 1)
                    if lat:
                        dve.wait_ge(sem("dn_qexp"), 4 * d + i - 1)
                        V.tensor_tensor(ATTN, Y, ps(3, 0, 512), ALU.mult).then_inc(sem("dn_q"), 1)
                        V.tensor_tensor(h4(QG), proj[:, DNQ:DNQ + 4, tc], h4(ps(4, 0, 512)), ALU.mult).then_inc(sem("dn_q"), 1)
                    eye = ident.unsqueeze(1).to_broadcast([P, 4, P])
                    dve.wait_ge(sem("dn_y_in"), LEVELS * u + 1)
                    V.tensor_tensor(h4(X), eye, h4(ps(5, 0, 512)), ALU.add).then_inc(sem("dn_x"), 1)
                    dve.wait_ge(sem("dn_level"), LEVELS * u + 1)
                    V.tensor_tensor(h4(XT), eye, h4(LV[0]), ALU.add).then_inc(sem("dn_x"), 1)
                    for k in range(1, LEVELS):
                        dve.wait_ge(sem("dn_z_in"), 6 * u + k)
                        dve.wait_ge(sem("dn_x"), 2 * (LEVELS * u + k))
                        V.tensor_tensor(X, X, ps(6, 0, 512), ALU.add).then_inc(sem("dn_x"), 1)
                        V.tensor_tensor(XT, XT, ps(7, 0, 512), ALU.add).then_inc(sem("dn_x"), 1)
                    dve.wait_ge(sem("dn_u_in"), u + 1)
                    V.tensor_copy(U, ps(6, 0, 512)).then_inc(sem("dn_u"), 1)
                    if lat:
                        dve.wait_ge(sem("dn_o_in"), 4 * d + i - 1)
                        y = hT[:, 4:8, tc]
                        if d == 0:
                            V.tensor_copy(y, h4(ps(7, 0, 512))).then_inc(sem("dn_o"), 1)
                        else:
                            V.tensor_tensor(y, y, h4(ps(7, 0, 512)), ALU.add).then_inc(sem("dn_o"), 1)
                    dve.wait_ge(sem("dn_s_in"), u + 1)
                    if i == 0:
                        V.tensor_copy(ST, ps(0, 0, 512)).then_inc(sem("dn_state"), 1)
                    else:
                        dve.wait_ge(sem("dn_state"), u)
                        for h in range(HEADS):
                            s = slice(P * h, P * h + P)
                            last = V.scalar_tensor_tensor(out=ST[:, s], in0=ST[:, s], scalar=endb[:, c, 4 * d + h:4 * d + h + 1],
                                                          in1=ps(0, P * h, P * h + P), op0=ALU.mult, op1=ALU.add)
                        last.then_inc(sem("dn_state"), 1)

            def gate_y(layer, first, c0, stage):
                for h in range(HEADS):
                    dve.wait_ge(sem(f"hnorm_{stage}"), h + 1)
                    dve.wait_ge(sem(f"out_gate{layer}"), h + 1)
                    V.tensor_tensor(hT[:, 4 + h, c0:T], hT[:, 4 + h, c0:T], proj[:, first + h, c0:T], ALU.mult).then_inc(sem(f"y_gated{layer}"), 1)

            def added(stage, layer, ga, c0, signal):
                j0, n, per, done = PLAN[f"{stage}{layer}"]
                if stage == "out":
                    for b in range(8):
                        dve.wait_ge(sem("products"), done + b + 1)
                        add_in(b, 2 * (b % 4), layer, ga, c0, signal)
                else:
                    with dve.Fori(0, 4) as i:
                        for b in range(2):
                            dve.wait_ge(sem("products"), 4 * i + (done + 2 * b + 2))
                            add_in(2 * i + b, 2 * b, layer, ga, c0, signal)

            def up(layer, c0):
                _, _, _, done = PLAN[f"up{layer}"]
                w = T - c0

                def body(f, i):
                    dve.wait_ge(sem("products"), 8 * i + (done + 4 * (f // 2) + 2 + f % 2 + 1))
                    dve.wait_ge(sem(f"ffn_silu{layer}"), 4 * i + (f + 1))
                    V.tensor_tensor(proj[:, bass.ds(4 * i + f, 1), c0:T].rearrange("p a t -> p (a t)"), sq[:, f % 2, 0:w],
                                    ps(4 + 2 * (f % 2), 0, w), ALU.mult).then_inc(sem(f"ffn_act{layer}"), 1)

                with dve.Fori(0, FC // 4) as i:
                    for f in range(4):
                        body(f, i)
                for f in range(FC % 4):
                    body(f, FC // 4)

            for layer in range(2):
                c0 = 0 if layer == 0 else CTX
                if layer == 0:
                    dve.wait_ge(sem("mod_ready"), 1)
                norm(f"mix{layer}", 0, gmT[:, layer, 0])
                project_out(layer)
                output = att_output(layer)
                if layer == 0:
                    gate_rows(0)
                    dve.wait_ge(sem("proj_moved0"), 24)
                    rope(0)
                    attention(0)
                    dve.wait_ge(sem("products"), PLAN["out0"][3])
                    modulation(16, 96, [(0, 1), (1, 0), (1, 1)])
                    head_norm("da")
                    rows_even()
                    mlstm()
                    head_norm("ml")
                    gate_y(0, MLO, 0, "ml")
                else:
                    dve.wait_ge(sem("proj_moved1"), 22)
                    conv()
                    head_norm("l2")
                    gate_rows(1)
                    head_norm("qk")
                    dve.wait_ge(sem("hnorm_qk"), 5)
                    rope(1)
                    attention(1)
                    rows_odd()
                    deltanet()
                    head_norm("dn")
                    gate_y(1, DNZ, CTX, "dn")
                added("out", layer, GA1, c0, f"out_added{layer}")
                dve.wait_ge(sem(f"out_added{layer}"), 8 * (2 if c0 == 0 else 1))
                norm(f"ffn{layer}", c0, gmT[:, layer, 1])
                up(layer, c0)
                added("down", layer, GA2, c0, f"down_added{layer}")
                dve.wait_ge(sem(f"down_added{layer}"), 8 * (2 if c0 == 0 else 1))
            norm("final", CTX, None, vec_b[:, G_FINAL:G_FINAL + 8])


_INS = ["x", "c", "ctx", "c_ctx", "w_ada", "b_ada", "g_mix", "g_ffn", "w_in_e", "b_gate_e", "da_lam", "da_norm_g", "ml_norm_g",
        "w_out_e", "w_in_o", "qk_norm_g", "dn_conv", "dn_a_log", "dn_dt_bias", "dn_norm_g", "w_out_o", "w_gate", "w_up", "w_down",
        "g_final"]


def kernel(**inputs):
    import concourse.bacc as bacc
    from concourse.bass_utils import run_bass_kernel_spmd as run

    nc = bacc.Bacc("TRN2", target_bir_lowering=False, num_devices=1)
    arrays, args = {}, []
    tables = dict(zip(("const_f", "const_b", "rotary"), constant_tables()))
    for name in _INS + ["const_f", "const_b", "rotary"]:
        a = np.ascontiguousarray(inputs[name] if name in inputs else tables[name])
        arrays[f"in_{name}_dram"] = a
        args.append(nc.dram_tensor(f"in_{name}_dram", a.shape, mybir.dt.from_np(a.dtype), kind="ExternalInput").ap())
    args.append(nc.dram_tensor("out_0_dram", (1, LAT, D), F32, kind="ExternalOutput").ap())
    backbone(nc, *args)
    r = run(nc, [arrays], core_ids=[0])
    return r.results[0]["out_0_dram"]
```

```python
from contextlib import ExitStack

import numpy as np

import concourse.bass as bass
from concourse import mybir

F32 = mybir.dt.float32
BF16 = mybir.dt.bfloat16
F32R = mybir.dt.float32r
ACT = mybir.ActivationFunctionType
ALU = mybir.AluOpType
AX_X = mybir.AxisListType.X

P = 128
D = 1024
KD = D // P
CTX, LAT = 256, 512
T = CTX + LAT
NT = T // P
DFF = 2816
FC = DFF // P
GRID_W = 64
EPS = 1e-6
HEADS = 4
E_IN, O_IN = 3088, 2832
E_GATES, O_GATES = 3072, 2816
LAM_INIT = 0.2
BANK = 512
SLOTS = 4
GROW = 36
NEG = -1e30
ADA_COLS = 256
LEVELS = 7
DAQ, DAK, DAV, MLQ, MLK, MLV, MLO = 0, 4, 8, 12, 14, 16, 20
CQ, CK, CV, DNQ, DNK, DNV, DNZ = 0, 4, 5, 6, 10, 14, 18
G_MIX, G_FFN, G_FINAL, V_C, V_CCTX, G_DA, G_ML, G_DN, G_Q, G_K, CONV = 0, 16, 32, 40, 48, 56, 57, 58, 59, 60, 61
NVEC = CONV + 36
SH1, SC1, GA1, SH2, SC2, GA2 = 0, 8, 16, 24, 32, 40

C_ID, C_ONES, C_PERM, C_BLK, C_RST = 0, 128, 256, 384, 512
NCF = 640
B_ID, B_INCL, B_STRICT, B_LEVEL = 0, 128, 384, 640
NCB = B_LEVEL + LEVELS * 2 * P


def constant_tables():
    f = np.zeros((P, NCF), np.float32)
    i = np.arange(P)
    f[:, C_ID:C_ID + P] = np.eye(P)
    f[:, C_ONES:C_ONES + P] = 1.0
    f[i, C_PERM + (i ^ 16)] = 1.0
    f[:, C_BLK:C_BLK + P] = i[:, None] // 64 == i[None, :] // 64
    quarter = 16
    freqs = 10000.0 ** (-np.arange(quarter, dtype=np.float32) / np.float32(quarter))
    t = np.arange(LAT)
    pos = np.stack([t // GRID_W, t % GRID_W]).astype(np.float32)
    axis, second, idx = (i % 64) // 32, (i % 32) // 16, i % 16
    ang = pos[axis] * freqs.astype(np.float32)[idx][:, None]
    rot = np.concatenate([np.cos(ang), np.sin(ang) * np.where(second == 1, 1.0, -1.0)[:, None]], 1)
    f[0:32, C_RST:C_RST + P] = i != 0
    f[32:, C_RST:C_RST + P] = i != P - 1
    b = np.zeros((P, NCB), np.float32)
    b[:, B_ID:B_ID + P] = np.eye(P)
    s, q = i[:, None], i[None, :]
    for d in range(2):
        lo, hi = (s, q) if d == 0 else (q, s)
        b[:, B_INCL + d * P:B_INCL + (d + 1) * P] = np.where(lo <= hi, 0.0, NEG)
        b[:, B_STRICT + d * P:B_STRICT + (d + 1) * P] = np.where(lo < hi, 0.0, NEG)
        for k in range(LEVELS):
            w = 1 << k
            at = B_LEVEL + (k * 2 + d) * P
            b[:, at:at + P] = -1.0 * ((hi // w % 2 == 1) & (lo // w == hi // w - 1))
    return f, (b.view(np.uint32) >> 16).astype(np.uint16), rot.astype(np.float32)


STREAM = [("ada0", 8, 2), ("proj0", 12, 2), ("adb0", 16, 2), ("ada1", 24, 2), ("out0", 4, 2), ("up0", 22, 2), ("down0", 16, 1),
          ("proj1", 11, 2), ("out1", 4, 2), ("up1", 22, 2), ("down1", 16, 1)]


def stream_plan():
    plan, used_at, load, done = {}, [], 0, 0
    for name, n, per in STREAM:
        plan[name] = (load, n, per, done)
        used_at += [done + per * (j + 1) for j in range(n)]
        load += n
        done += per * n
    return plan, used_at


PLAN, USED_AT = stream_plan()
SPLIT = {}
for _name in ("proj0", "out0", "up0", "down0", "proj1", "out1", "up1", "down1"):
    SPLIT[_name] = sum(PLAN[n][1] * PLAN[n][2] for n in SPLIT)
DOWN_SPLIT = 16
HEAD_BASE = {"da": 0, "ml": HEADS, "l2": 2 * HEADS, "qk": 4 * HEADS, "dn": 4 * HEADS + 5}
SCALED_BASE = {"mix0": 0, "ffn0": 2 * KD, "mix1": 4 * KD, "ffn1": 6 * KD}
H_BASE = {"mix0": 0, "out0": 2 * KD, "ffn0": 3 * KD, "down0": 5 * KD, "mix1": 5 * KD + DOWN_SPLIT, "out1": 7 * KD + DOWN_SPLIT,
          "ffn1": 8 * KD + DOWN_SPLIT, "down1": 9 * KD + DOWN_SPLIT}


def backbone(nc, x, c, ctx_tok, c_ctx, w_ada, b_ada, g_mix, g_ffn, w_in_e, b_gate_e, da_lam, da_norm_g, ml_norm_g,
             w_out_e, w_in_o, qk_norm_g, dn_conv, dn_a_log, dn_dt_bias, dn_norm_g, w_out_o, w_gate, w_up, w_down,
             g_final, const_f, const_b, rotary, out):
    stack = ExitStack()
    with stack:
        def sb(name, shape, dt=F32):
            place[name] = -(-nc.sbuf_base // 32) * 32
            return stack.enter_context(nc.sbuf_tensor(name, shape, dt))

        place = {}

        def over(name, shape, of, floats=0):
            return nc.alloc_sbuf_tensor_at(name, shape, F32R, offset=place[of] + 4 * floats)

        named = {}

        def sem(name):
            if name not in named:
                named[name] = stack.enter_context(nc.semaphore(name))
            return named[name]

        xT = sb("xT", [P, KD, T])
        hT = sb("hT", [P, KD, T])
        proj = sb("proj", [P, 24, T])
        tok = sb("tok", [P, 10 * T])
        ring = sb("ring", [P, SLOTS, 2048])
        cf = sb("cf", [P, NCF])
        cb_bits = sb("cb_bits", [P, NCB], mybir.dt.uint16)
        cb = cb_bits[:].bitcast(BF16)
        sq = sb("sq", [P, 2, T])
        rs = sb("rs", [P, 2, T])
        vec_a = sb("vec_a", [P, 96])
        vec_b = sb("vec_b", [P, NVEC])
        modT = sb("modT", [P, 2, 48, 2])
        gmT = sb("gmT", [P, 2, 2, KD, 2])
        silu_c = sb("silu_c", [P, KD, 2])
        gate_in = sb("gate_in", [P, 2, KD, 16])
        gate_b = sb("gate_b", [GROW, 8])
        cols = sb("cols", [P, 4, NT, 8])
        endr = sb("endr", [GROW, 6, 8])
        endx = sb("endx", [GROW, NT, GROW])
        endb = sb("endb", [P, NT, 8])
        small = sb("small", [P, 32])
        hT_lo = over("hT_lo", [P, KD, T], "hT")
        h_hi = over("h_hi", [P, KD, T], "tok")
        ring_lo = over("ring_lo", [P, SLOTS, KD, 256], "ring")
        w_hi = [over("w_hi_a", [P, KD, P], "tok", KD * T), over("w_hi_b", [P, KD, P], "rs")]
        proj_lo = over("proj_lo", [P, 24, T], "proj")
        wd_hi = [over("wd_hi_a", [P, FC // 2, P], "tok", KD * T), over("wd_hi_b", [P, DOWN_SPLIT - FC // 2, P], "rs")]
        ring_lo_flat = ring_lo[:].rearrange("p s k n -> p s (k n)")

        def act_hi(k):
            return hT_lo[:, k, :] if k < KD else h_hi[:, k - KD, :]

        PS = stack.enter_context(nc.psum_tensor("PS", [P, 8 * BANK], F32))

        ident, ones, perm, blk = (cf[:, a:a + P] for a in (C_ID, C_ONES, C_PERM, C_BLK))
        rot_at = [proj[:, b:b + 2, :].rearrange("p a t -> p (a t)")[:, 0:2 * LAT] for b in (9, 16)]
        ident_b = cb[:, B_ID:B_ID + P]
        incl = [cb[:, B_INCL + d * P:B_INCL + (d + 1) * P] for d in range(2)]
        strict = [cb[:, B_STRICT + d * P:B_STRICT + (d + 1) * P] for d in range(2)]
        tok_e = tok[:, 0:NT * 1280].rearrange("p (t n) -> p t n", t=NT)
        tok_o = tok[:, 0:NT * 1152].rearrange("p (t n) -> p t n", t=NT)
        tok_free = tok[:, NT * 1152:NT * 1152 + T]
        x_tok = proj[:, 0:8, :].rearrange("p a b -> p (a b)").rearrange("p (t n) -> p t n", t=NT)
        out_tok = proj[:, 0:6, :].rearrange("p a b -> p (a b)")[:, 0:4 * D].rearrange("p (t n) -> p t n", t=4)
        vec_rows = proj[:, 8, 0:256].rearrange("p (a n) -> p a n", a=2)
        gate_w = [b[:, 0:KD * 2 * GROW].rearrange("p (k a n) -> p k a n", k=KD, a=2) for b in (proj[:, 8, :], tok_free)]
        lam_in = proj[:, 10, 0:256].rearrange("p (a n) -> p a n", a=4)
        lam_tmp = proj[:, 10, 256:384].rearrange("p (a n) -> p a n", a=2)

        def bank(b, n=BANK):
            return PS[:, b * BANK:b * BANK + n]

        def ps(b, lo, hi):
            return PS[:, b * BANK + lo:b * BANK + hi]

        def sel(d, j):
            r = 32 * d + j
            return cf[0:GROW, C_ID + r:C_ID + r + 1].to_broadcast([GROW, P])

        def slot(i):
            return proj[:, i, :]

        def ada_row(n):
            return sq[0:2, n % 2, 0:256]

        class Att:
            def __init__(self, layer):
                self.layer = layer
                if layer == 0:
                    self.maps, self.vd = 2, P
                    self.tiles = [(h, q) for h in range(HEADS) for q in range(NT)]
                    self.E = [[slot(8), slot(9)], [slot(10), slot(11)]]
                    self.PT = [slot(18), slot(19)]
                else:
                    self.maps, self.vd = 1, 64
                    self.tiles = [(h, q) for h in range(8) for q in range(2, NT)]
                    self.E = [[slot(15)], [slot(16)]]
                    self.PT = [slot(17), tok_free]

            def keys(self, i):
                return T if self.tiles[i][1] >= 2 else CTX

            def q(self, i, m):
                h, q = self.tiles[i]
                if self.layer == 0:
                    return proj[64 * m:64 * m + 64, DAQ + h, P * q:P * q + P]
                r = 64 * (h % 2)
                return proj[r:r + 64, CQ + h // 2, P * q:P * q + P]

            def k(self, i, m, lo, hi):
                h, _ = self.tiles[i]
                if self.layer == 0:
                    return proj[64 * m:64 * m + 64, DAK + h, lo:hi]
                r = 64 * (h % 2)
                return proj[r:r + 64, 22 + h // 4, lo:hi]

            def v(self, i, kt):
                h, _ = self.tiles[i]
                if self.layer == 0:
                    return tok_e[:, kt, P * h:P * h + P]
                return tok_o[:, kt, 1024 + 64 * (h // 4):1024 + 64 * (h // 4) + 64]

            def rows(self, i):
                h, _ = self.tiles[i]
                return (0, P) if self.layer == 0 else (64 * (h % 2), 64 * (h % 2) + 64)

            def y(self, i):
                h, q = self.tiles[i]
                lo, hi = self.rows(i)
                block_ = hT[lo:hi, h if self.layer == 0 else h // 2, :]
                return block_[:, P * q:P * q + P] if q < 2 else block_[:, CTX + q - 2:T:LAT // P]

        def head_norm_items(stage):
            if stage == "da":
                return [(hT[:, h, :], ones, 1.0 / P, small[:, 4:5], hT[:, h, :], T) for h in range(HEADS)]
            if stage == "ml":
                return [(hT[:, 4 + h, :], ones, 1.0 / P, vec_b[:, G_ML:G_ML + 1], hT[:, 4 + h, :], T) for h in range(HEADS)]
            if stage == "qk":
                its = [(proj[:, CQ + b, CTX:T], blk, 1.0 / 64, vec_b[:, G_Q:G_Q + 1], proj[:, CQ + b, CTX:T], LAT) for b in range(4)]
                return its + [(proj[:, CK, :], blk, 1.0 / 64, vec_b[:, G_K:G_K + 1], proj[:, CK, :], T)]
            if stage == "l2":
                return [(proj[:, b, :], ones, 1.0, P ** -0.5 if b < DNK else 1.0, proj[:, b, :], T) for b in range(DNQ, DNV)]
            return [(hT[:, 4 + h, CTX:T], ones, 1.0 / P, vec_b[:, G_DN:G_DN + 1], hT[:, 4 + h, CTX:T], LAT) for h in range(HEADS)]

        UNIT_NORM = {**{u: ("da", u) for u in range(HEADS)}, **{HEADS + 1 + h: ("ml", h) for h in range(HEADS)}}

        def transposes(stage):
            if stage == "even":
                its = []
                for t in range(NT):
                    for first, n, at in ((DAV, 4, 0), (MLV, 4, 512), (MLK, 2, 1024)):
                        its.append(([proj[:, first + j, P * t:P * t + P] for j in range(n)], tok_e[:, t, at:at + P * n]))
                return its
            its = []
            for t in range(NT):
                for first, n, at in ((DNV, 4, 0), (DNK, 4, 512), (CV, 1, 1024)):
                    its.append(([proj[:, first + j, P * t:P * t + P] for j in range(n)], tok_o[:, t, at:at + P * n]))
            return its

        ROPE = {0: [DAQ + j for j in range(8)], 1: [CQ + j for j in range(5)]}

        ORDER = [[0, 1, 2, 3, 4, 5], [1, 0, 5, 4, 3, 2]]
        rowI, rowF = proj[0:GROW, 16, :], proj[0:GROW, 17, :]
        er = [proj[0:GROW, i, :] for i in range(8)]
        e_logf, e_m, e_b, e_ib, e_A, e_inter, e_em, e_t = er
        o_rst = proj[0:GROW, 15, :]
        o_rowI, o_rowF = proj[0:GROW, 5, :], proj[0:GROW, 14, :]
        o_g, o_gb, o_eg, o_t = sq[0:GROW, 0, :], sq[0:GROW, 1, :], rs[0:GROW, 0, :], rs[0:GROW, 1, :]
        pexp, pm, qt, den = slot(8), slot(9), slot(10), slot(11)
        cst = proj[:, 18:20, :].rearrange("p a b -> p (a b)").rearrange("p (c n) -> p c n", c=NT)
        kw = sq[:, 0, 0:NT * 64].rearrange("p (c n) -> p c n", c=NT)
        runA = proj[:, 0:6, :].rearrange("p a b -> p (a b)")
        runB = proj[:, 14:18, :].rearrange("p a b -> p (a b)")
        runC = proj[:, 22:24, :].rearrange("p a b -> p (a b)")
        bufs = [r[:, 512 * i:512 * i + 512] for r, n in ((runA, 9), (runB, 6), (runC, 3)) for i in range(n)]
        ring_bufs = [ring[:, i // 4, 512 * (i % 4):512 * (i % 4) + 512] for i in range(16)]
        by_head = [[b.rearrange("p (h n) -> p h n", h=4) for b in bs] for bs in (bufs + [tok_free[:, 0:512]], ring_bufs)]
        by_head[1] += [hT[:, 4:8, 0:P], hT[:, 4:8, P:2 * P], proj[:, DNZ:DNZ + 4, 0:P]]

        class Stream:

            def __init__(self, d):
                b = by_head[d]
                self.AT, self.LV, self.X, self.XT, self.Y, self.ATTN, self.KB, self.VB = b[0], b[1:8], b[8], b[9], b[10], b[11], b[12], b[13]
                self.WT, self.KDC, self.U, self.ST, self.QG = b[14:19]
                self.d, self.at = d, 4 * d

            def ps(self, b):
                return h4(ps(self.at + b, 0, 512))

            def head(self, b, h):
                return ps(self.at + b, P * h, P * h + P)

            def chunk(self, i):
                return ORDER[self.d][i]

            def tokens(self, i):
                c = ORDER[self.d][i]
                return slice(P * c, P * c + P)

        STEPS = NT
        LAT_STEP = CTX // P

        def nth(i, d, events=1, e=0):
            return 2 * (events * i + e) + d + 1


        resets = cf[0:GROW, C_RST:C_RST + P].unsqueeze(1).to_broadcast([GROW, NT, P])

        def h4(ap):
            return ap.rearrange("p (h n) -> p h n", h=4)

        weights = {"proj0": w_in_e[0], "proj1": w_in_o[0], "out0": w_out_e[0], "out1": w_out_o[0]}
        weights["ada0"], weights["adb0"], weights["ada1"] = w_ada[0][:, 0:16 * P], w_ada[0][:, 16 * P:], w_ada[1]

        def segments(c0):
            return [(0, 512), (512, T)] if c0 == 0 else [(c0, T)]

        block = stack.enter_context(nc.Block())

        @block.sync
        def _(sp):
            sp.dma_start(cf[:], const_f).then_inc(sem("const_in"), 16)
            sp.dma_start(vec_rows[0:96, 0, :], b_ada.rearrange("l (m p) -> (l m) p", p=P)).then_inc(sem("vec_in"), 16)
            for at, src in ((G_MIX, g_mix.rearrange("l (m p) -> (l m) p", p=P)), (G_FFN, g_ffn.rearrange("l (m p) -> (l m) p", p=P)),
                            (G_FINAL, g_final.rearrange("(m p) -> m p", p=P)), (V_C, c.rearrange("b (m p) -> (b m) p", p=P)),
                            (V_CCTX, c_ctx.rearrange("(m p) -> m p", p=P)), (G_DA, da_norm_g), (G_ML, ml_norm_g), (G_DN, dn_norm_g),
                            (CONV, dn_conv.rearrange("o t (m p) -> (o t m) p", p=P))):
                sp.dma_start(vec_rows[at:at + src.shape[0], 1, :], src).then_inc(sem("vec_in"), 16)
            for half in range(2):
                sp.dma_start(vec_rows[G_Q:G_Q + 2, 1, 64 * half:64 * half + 64], qk_norm_g[0]).then_inc(sem("vec_in"), 16)
            sp.dma_start(x_tok[:, 0:2, :], ctx_tok[0].rearrange("(t p) d -> p t d", p=P)).then_inc(sem("tok_in"), 16)
            sp.dma_start(x_tok[:, 2:6, :], x[0].rearrange("(t p) d -> p t d", p=P)).then_inc(sem("tok_in"), 16)
            sp.dma_start(cb_bits[:], const_b).then_inc(sem("const_in"), 16)
            for l, w, at in ((0, w_in_e, E_GATES), (1, w_in_o, O_GATES)):
                sp.dma_start(gate_in[:, l], w[0].rearrange("(k p) n -> p k n", p=P)[:, :, at:at + 16]).then_inc(sem("gates_in"), 16)
            sp.dma_start(lam_in, da_lam.partition_broadcast(P).rearrange("p o a n -> p (o a) n")).then_inc(sem("gates_in"), 16)
            sp.wait_ge(sem("cleared"), 1)
            col = lambda ap: ap.rearrange("(p q) -> p q", q=1)
            for d in range(2):
                r = slice(32 * d, 32 * d + 4)
                sp.dma_start(gate_b[r, 0:1], col(b_gate_e[0, 8 * d:8 * d + 4])).then_inc(sem("gates_in"), 16)
                sp.dma_start(gate_b[r, 1:2], col(b_gate_e[0, 8 * d + 4:8 * d + 8])).then_inc(sem("gates_in"), 16)
                sp.dma_start(gate_b[r, 2:3], col(dn_dt_bias[0, d])).then_inc(sem("gates_in"), 16)
                sp.dma_start(gate_b[r, 3:4], col(dn_a_log[0, d])).then_inc(sem("gates_in"), 16)

            def load(stage, k, s):
                if stage[:-1] == "down":
                    n, half = k
                    src = w_down[int(stage[-1])].rearrange("(k p) n -> p k n", p=P)[:, 11 * half:11 * half + 11, bass.ds(128 * n, 128)]
                    dst = ring[:, s, 0:11 * 128].rearrange("p (k n) -> p k n", k=11)
                elif stage[:-1] == "up":
                    n, which = k
                    src = (w_gate, w_up)[which][int(stage[-1])].rearrange("(k p) n -> p k n", p=P)[:, :, bass.ds(256 * n, 256)]
                    dst = ring[:, s, :].rearrange("p (k n) -> p k n", k=KD)
                else:
                    src = weights[stage].rearrange("(k p) n -> p k n", p=P)[:, :, bass.ds(256 * k, 256)]
                    dst = ring[:, s, :].rearrange("p (k n) -> p k n", k=KD)
                sp.dma_start(dst, src).then_inc(sem(f"weights_in{s}"), 16)

            def part(stage, i, k):
                return (2 * i + k // 2, k % 2) if stage[:-1] in ("up", "down") else 4 * i + k

            def stream(stage):
                j0, n, per, done = PLAN[stage]
                for k in range(min(4, n)):
                    if j0 + k >= SLOTS:
                        sp.wait_ge(sem("products"), USED_AT[j0 + k - SLOTS])
                    load(stage, part(stage, 0, k), (j0 + k) % SLOTS)
                if n // 4 > 1:
                    with sp.Fori(1, n // 4) as i:
                        for k in range(4):
                            sp.wait_ge(sem("products"), 4 * per * i + (done + per * (k - 3)))
                            load(stage, part(stage, i, k), (j0 + k) % SLOTS)
                for k in range(max(4, n // 4 * 4), n):
                    sp.wait_ge(sem("products"), USED_AT[j0 + k - SLOTS])
                    load(stage, part(stage, n // 4, k % 4), (j0 + k) % SLOTS)

            for stage, _, _ in STREAM:
                if stage == "out1":
                    sp.wait_ge(sem("dn_s_in"), 2 * STEPS)
                stream(stage)
                if stage[:-1] == "proj":
                    layer = int(stage[-1])
                    sp.wait_ge(sem("moved_odd" if layer else "moved_even"), 3 * NT)
                    sp.dma_start(rot_at[layer], rotary).then_inc(sem("rotary_in"), 16)
                if stage == "proj1":
                    sp.wait_ge(sem("rope_done1"), 5)
                    for g in range(2):
                        for half in range(2):
                            sp.dma_start(proj[64 * half:64 * half + 64, 22 + g, :], proj[64 * g:64 * g + 64, CK, :]).then_inc(sem("keys_spread"), 16)
            sp.wait_ge(sem("out_moved"), 8)
            sp.dma_start(out[0].rearrange("(t p) d -> p t d", p=P), out_tok).then_inc(sem("stored"), 16)
            sp.wait_ge(sem("stored"), 16)

        @block.gpsimd
        def _(pool):
            nc.gpsimd.memset(gate_b[:], 0.0).then_inc(sem("cleared"), 1)

            def low_parts(stage):
                j0, n, _, _ = PLAN[stage]

                def body(q, i):
                    slot_, half = (j0 + q // 2) % SLOTS, q % 2
                    pool.wait_ge(sem("w_hi"), 8 * i + (SPLIT[stage] + q + 1))
                    cols_ = slice(P * half, P * half + P)
                    raw = ring[:, slot_, :].rearrange("p (k n) -> p k n", k=KD)[:, :, cols_]
                    nc.gpsimd.tensor_tensor(ring_lo[:, slot_, :, cols_], raw, w_hi[half][:], ALU.subtract).then_inc(sem("w_lo"), 1)

                if n // 4 > 1:
                    with pool.Fori(0, n // 4) as i:
                        for q in range(8):
                            body(q, i)
                for q in range(n // 4 * 8 if n // 4 > 1 else 0, 2 * n):
                    body(q % 8, q // 8)

            def low_parts_down(stage):
                j0, n, _, _ = PLAN[stage]
                with pool.Fori(0, n // 4) as i:
                    for q in range(4):
                        w = wd_hi[q % 2]
                        size = P * w.shape[1]
                        pool.wait_ge(sem("w_hi"), 4 * i + (SPLIT[stage] + q + 1))
                        slot_ = (j0 + q) % SLOTS
                        nc.gpsimd.tensor_tensor(ring_lo_flat[:, slot_, 0:size], ring[:, slot_, 0:size], w[:].rearrange("p k n -> p (k n)"),
                                                ALU.subtract).then_inc(sem("w_lo"), 1)

            def padded_gates(layer):
                if layer == 0:
                    pool.wait_ge(sem("moved_even"), 3 * NT)
                pool.wait_ge(sem("gates_in"), 16 * 11)
                nc.gpsimd.memset(gate_w[layer], 0.0).then_inc(sem("gate_w"), 1)
                pool.wait_ge(sem("gate_w"), 5 * layer + 1)
                for kind in range(2):
                    for d in range(2):
                        at = 8 * d + 4 * kind
                        nc.gpsimd.tensor_copy(gate_w[layer][:, :, kind, 32 * d:32 * d + 4], gate_in[:, layer, :, at:at + 4]).then_inc(sem("gate_w"), 1)

            low_parts("proj0")
            padded_gates(0)
            low_parts("out0")
            low_parts("up0")
            low_parts_down("down0")
            low_parts("proj1")
            pool.wait_ge(sem("products"), PLAN["proj1"][3] + 22)
            for k in range(KD):
                nc.gpsimd.tensor_tensor(hT[:, k, :], h_hi[:, k, :], hT_lo[:, k, :], ALU.add).then_inc(sem("h_back"), 1)
            padded_gates(1)

            streams = [Stream(d) for d in range(2)]
            pool.wait_ge(sem("dn_cols"), 1)
            pool.wait_ge(sem("moved_odd"), 3 * NT)
            for i in range(STEPS):
                for k in range(LEVELS):
                    for d, st in enumerate(streams):
                        if k == 0:
                            pool.wait_ge(sem("dn_at"), nth(i, d))
                        at = B_LEVEL + (k * 2 + d) * P
                        nc.gpsimd.tensor_tensor(st.LV[k], st.AT, cb[:, at:at + P].unsqueeze(1).to_broadcast([P, 4, P]),
                                                ALU.mult).then_inc(sem("dn_level"), 1)
                for d, st in enumerate(streams):
                    c = st.chunk(i)
                    for dst, at, which in ((st.KB, 512, 1), (st.VB, 0, 0), (st.KDC, 512, 2)):
                        last = nc.gpsimd.tensor_tensor(dst, h4(tok_o[:, c, at:at + 512]),
                                                       cols[:, which, c, 4 * d:4 * d + 4].unsqueeze(2).to_broadcast([P, 4, P]), ALU.mult)
                    last.then_inc(sem("dn_scaled"), 1)
            low_parts("out1")
            low_parts("up1")
            low_parts_down("down1")

        @block.tensor
        def _(pe):
            mm, tr = nc.tensor.matmul, nc.tensor.transpose
            pe.wait_ge(sem("const_in"), 32)
            pe.wait_ge(sem("vec_in"), 16 * 12)
            tr(ps(0, 0, 96), vec_rows[0:96, 0, :], ident[0:96, 0:96]).then_inc(sem("vec_turned"), 1)
            tr(ps(1, 0, NVEC), vec_rows[0:NVEC, 1, :], ident[0:NVEC, 0:NVEC]).then_inc(sem("vec_turned"), 1)
            pe.wait_ge(sem("tok_in"), 32)
            for k in range(KD):
                if k >= 2:
                    pe.wait_ge(sem("x_moved"), k - 1)
                for t in range(NT):
                    last = tr(ps(2 + 2 * (k % 2), P * t, P * t + P), x_tok[:, t, P * k:P * k + P], ident)
                last.then_inc(sem("x_turned"), 1)

            def arrived(j):
                pe.wait_ge(sem(f"weights_in{j % SLOTS}"), 16 * (j // SLOTS + 1))

            pe.wait_ge(sem("silu_c"), 1)
            ada_loads = [PLAN[stage][0] + j for stage in ("ada0", "adb0", "ada1") for j in range(PLAN[stage][1])]

            def ada_load(n, b):
                j = ada_loads[n]
                arrived(j)
                for kk in range(KD):
                    last = mm(PS[0:2, b * BANK:b * BANK + 256], silu_c[:, kk, :], ring[:, j % SLOTS, 256 * kk:256 * kk + 256],
                              start=kk == 0, stop=kk == KD - 1)
                last.then_inc(sem("products"), 2)

            def ada_turn(n):
                pe.wait_ge(sem("ada_rows"), n + 1)
                for half in range(2):
                    last = tr(ps(6, ADA_COLS + 4 * n + 2 * half, ADA_COLS + 4 * n + 2 * half + 2), ada_row(n)[:, P * half:P * half + P],
                              ident[0:2, 0:2])
                last.then_inc(sem("ada_turned"), 1)

            for n in range(8):
                if n >= 2:
                    ada_turn(n - 2)
                ada_load(n, n % 2)
            ada_turn(6)
            ada_turn(7)

            def ready(tag, parts):
                return [H_BASE[tag] + parts * (k + 1) for k in range(KD)]

            def norm_sums(tag, c0):
                for k in range(KD):
                    pe.wait_ge(sem("squared"), norm_no[0] * KD + k + 1)
                    for lo, hi in segments(c0):
                        last = mm(PS[:, lo - c0:hi - c0], ones, sq[:, k % 2, lo:hi], start=k == 0, stop=k == KD - 1)
                    last.then_inc(sem("squares_summed"), 1)
                norm_no[0] += 1

            norm_no = [0]

            def split_product(stage, q, i, a, c0, h_ready=None):
                pe.wait_ge(sem("w_lo"), 8 * i + (SPLIT[stage] + q + 1))
                slot_, half = (PLAN[stage][0] + q // 2) % SLOTS, q % 2
                for kk in range(KD):
                    if h_ready is not None:
                        pe.wait_ge(sem("h_ready"), h_ready[kk])
                    high, low = w_hi[half][:, kk, :], ring_lo[:, slot_, kk, P * half:P * half + P]
                    passes = ((high, h_hi), (high, hT_lo), (low, h_hi))
                    for n, (w, moving) in enumerate(passes):
                        for lo, hi in segments(c0):
                            last = mm(ps(a, lo - c0, hi - c0), w, moving[:, kk, lo:hi], start=kk == 0 and n == 0,
                                      stop=kk == KD - 1 and n == len(passes) - 1)
                last.then_inc(sem("products"), 1)

            def rounds(stage, body):
                total = 2 * PLAN[stage][1]
                for q in range(min(8, total)):
                    body(q, 0)
                if total // 8 > 1:
                    with pe.Fori(1, total // 8) as i:
                        for q in range(8):
                            body(q, i)
                for q in range(max(total // 8 * 8, 8), total):
                    body(q % 8, q // 8)

            def project(stage, c0, h_ready, free, per=1):

                def body(q, i):
                    if isinstance(i, int):
                        if 8 * i + q >= 4:
                            pe.wait_ge(sem(free), per * (8 * i + q - 3))
                    else:
                        pe.wait_ge(sem(free), 8 * per * i + per * (q - 3))
                    first = isinstance(i, int) and 8 * i + q == 0
                    split_product(stage, q, i, 2 * (q % 4), c0, h_ready if first else None)
                rounds(stage, body)

            def gates(layer, pieces=range(4)):
                for piece in pieces:
                    kind, half = divmod(piece, 2)
                    if piece == 0:
                        pe.wait_ge(sem("gate_w"), 5 * (layer + 1))
                    for kk in range(KD // 2 * half, KD // 2 * (half + 1)):
                        for lo, hi in segments(0):
                            last = mm(PS[0:GROW, (4 + 2 * kind) * BANK + lo:(4 + 2 * kind) * BANK + hi], gate_w[layer][:, kk, kind, :],
                                      hT[:, kk, lo:hi], start=kk == 0, stop=kk == KD - 1)
                    if half == 1:
                        last.then_inc(sem("gate_rows"), 1)

            def turn(stage):
                for i, (srcs, _) in enumerate(transposes(stage)):
                    if i >= 4:
                        pe.wait_ge(sem(f"moved_{stage}"), i - 3)
                    for j, src in enumerate(srcs):
                        last = tr(ps(i % 4, P * j, P * j + P), src, ident)
                    last.then_inc(sem(f"turned_{stage}"), 1)

            def head_norm_sums(stage, ahead=None):
                for i, (_, mat, _, _, _, n) in enumerate(head_norm_items(stage)):
                    if ahead is not None:
                        ahead(i)
                    pe.wait_ge(sem("hsq"), HEAD_BASE[stage] + i + 1)
                    if i >= 2:
                        pe.wait_ge(sem("hms"), HEAD_BASE[stage] + i - 1)
                    for lo, hi in ((0, 512), (512, n)):
                        if hi > lo:
                            last = mm(ps(2 * (i % 2), lo, hi), mat, sq[:, i % 2, lo:hi], start=True, stop=True)
                    last.then_inc(sem("hsum"), 1)

            def unit_norm_sums(u):
                if u not in UNIT_NORM:
                    return
                stage, i = UNIT_NORM[u]
                pe.wait_ge(sem("hsq"), HEAD_BASE[stage] + i + 1)
                for lo, hi in segments(0):
                    last = mm(ps(6, lo, hi), ones, sq[:, 1, lo:hi], start=True, stop=True)
                last.then_inc(sem("hsum"), 1)

            def rope(layer):
                for i, b in enumerate(ROPE[layer]):
                    if i >= 2:
                        pe.wait_ge(sem(f"rope_done{layer}"), i - 1)
                    mm(ps(4 + i % 2, 0, LAT), perm, proj[:, b, CTX:T], start=True, stop=True).then_inc(sem(f"rope_swapped{layer}"), 1)

            def attention(layer):
                a = Att(layer)
                n = len(a.tiles)

                def scores(i):
                    for m in range(a.maps):
                        b = 2 * m if a.maps == 2 else 2 * (i % 2)
                        if a.maps == 2 and i >= 1:
                            pe.wait_ge(sem(f"att_exp{layer}"), 2 * (i - 1) + m + 1)
                        if a.maps == 1 and i >= 2:
                            pe.wait_ge(sem(f"att_exp{layer}"), i - 1)
                        nk = a.keys(i)
                        for lo, hi in ((0, min(512, nk)), (512, nk)):
                            if hi > lo:
                                last = mm(ps(b, lo, hi), a.q(i, m), a.k(i, m, lo, hi), start=True, stop=True)
                        last.then_inc(sem(f"att_scores{layer}"), 1)

                def values(i):
                    nk = a.keys(i) // P
                    pe.wait_ge(sem(f"att_pt{layer}"), i + 1)
                    if i >= 1:
                        pe.wait_ge(sem(f"att_y{layer}"), i)
                    lo, hi = a.rows(i)
                    for kt in range(nk):
                        last = mm(PS[lo:hi, 7 * BANK:7 * BANK + P], a.v(i, kt), a.PT[i % 2][:, P * kt:P * kt + P],
                                  start=kt == 0, stop=kt == nk - 1)
                    last.then_inc(sem(f"att_out{layer}"), 1)

                def later_ada(j):
                    if 0 < j <= 40:
                        ada_turn(8 + j - 1)
                    if j < 40:
                        ada_load(8 + j, 6)

                scores(0)
                for i in range(n):
                    if i + 1 < n:
                        scores(i + 1)
                    if i >= 1:
                        values(i - 1)
                    if layer == 0:
                        later_ada(2 * i)
                    nk = a.keys(i) // P
                    pe.wait_ge(sem(f"att_probs{layer}"), i + 1)
                    if i >= 1:
                        pe.wait_ge(sem(f"att_pt{layer}"), i)
                    for kt in range(nk):
                        last = tr(ps(4, P * kt, P * kt + P), a.E[i % 2][0][:, P * kt:P * kt + P], ident)
                    last.then_inc(sem(f"att_turned{layer}"), 1)
                    if layer == 0:
                        later_ada(2 * i + 1)
                values(n - 1)

            def row_columns(layer, rows):
                pe.wait_ge(sem(f"rows_ready{layer}"), 1)
                for w, row in enumerate(rows):
                    for ch in range(NT):
                        last = tr(PS[:, w * BANK + GROW * ch:w * BANK + GROW * ch + GROW], row[:, P * ch:P * ch + P], ident[0:GROW, 0:GROW])
                last.then_inc(sem(f"columns_turned{layer}"), 1)

            def ends(layer, w):
                pe.wait_ge(sem(f"ends_spread{layer}"), w + 1)
                mm(PS[:, (2 + w) * BANK:(2 + w) * BANK + NT * GROW], ones[0:GROW, :], endx[:].rearrange("p a b -> p (a b)"),
                   start=True, stop=True).then_inc(sem(f"ends_out{layer}"), 1)

            def spread(b, row, d, j, masks=None):
                for lo, hi in segments(0):
                    last = mm(ps(b, lo, hi), sel(d, j), row[:, lo:hi], start=True, stop=masks is None)
                    if masks is not None:
                        n = (hi - lo) // P
                        last = mm(ps(b, lo, hi), ident_b, masks.unsqueeze(1).to_broadcast([P, n, P]), start=False, stop=True)
                return last

            def mlstm():
                pe.wait_ge(sem("ml_ready"), 1)
                for u in range(2 * HEADS):
                    d, h = divmod(u, HEADS)
                    r = 64 * (h % 2)
                    q, k = proj[r:r + 64, MLQ + h // 2, :], proj[r:r + 64, MLK + h // 2, :]
                    if u >= 1:
                        pe.wait_ge(sem("ml_den"), u)
                    spread(0, e_A, d, h, incl[d]).then_inc(sem("ml_pe"), 1)
                    if u >= 1:
                        pe.wait_ge(sem("ml_em_read"), u)
                    spread(4, e_inter, d, h).then_inc(sem("ml_pe"), 1)

                    def addition(i):
                        ch, b = ORDER[d][i], 6 + i % 2
                        pe.wait_ge(sem("ml_kw"), 6 * u + ch + 1)
                        if i >= 2 or u >= 1:
                            pe.wait_ge(sem("ml_state"), 5 * u + max(i - 1, 0))
                        mm(PS[r:r + 64, b * BANK:b * BANK + 128], kw[:, ch, :], tok_e[:, ch, 512 + P * h:512 + P * h + P], start=True, stop=True)
                        mm(PS[r:r + 64, b * BANK + 128:b * BANK + 256], kw[:, ch, :], ones, start=True, stop=True).then_inc(sem("ml_u"), 1)

                    addition(0)
                    addition(1)
                    if u >= 1:
                        pe.wait_ge(sem("ml_out"), u)
                    for ch in range(NT):
                        last = mm(ps(2, P * ch, P * ch + P), k[:, P * ch:P * ch + P], q[:, P * ch:P * ch + P], start=True, stop=True)
                    last.then_inc(sem("ml_pe"), 1)
                    for i in range(2, 5):
                        addition(i)
                    pe.wait_ge(sem("ml_state"), 5 * u + 5)
                    unit_norm_sums(u)
                    pe.wait_ge(sem("ml_probs"), u + 1)
                    pe.wait_ge(sem("ml_qt"), u + 1)
                    for which in range(2):
                        for i, ch in enumerate(ORDER[d]):
                            at = P * ch
                            o = ps(2 - 2 * which, at, at + P)
                            if i > 0:
                                mm(o, cst[r:r + 64, ch, 128 * which:128 * which + 128], qt[r:r + 64, at:at + P], start=True, stop=False)
                            w = ones if which else tok_e[:, ch, 512 + P * h:512 + P * h + P]
                            last = mm(o, w, pm[:, at:at + P], start=i == 0, stop=True)
                        last.then_inc(sem("ml_pe"), 1)
                    spread(4, e_em, d, h).then_inc(sem("ml_pe"), 1)

            def deltanet():
                pe.wait_ge(sem("dn_cols"), 1)
                streams = [Stream(d) for d in range(2)]
                heads = range(HEADS)
                for i in range(STEPS):
                    lat = i - LAT_STEP
                    for d, st in enumerate(streams):
                        tc = st.tokens(i)
                        if i >= 1:
                            pe.wait_ge(sem("dn_state"), nth(i - 1, d))
                        for h in heads:
                            mm(st.head(0, h), sel(d, h), o_gb[:, tc], start=True, stop=False)
                            mm(st.head(0, h), ident_b, strict[d], start=False, stop=True)
                        for h in heads:
                            k = proj[:, DNK + h, tc]
                            last = mm(st.head(1, h), k, k, start=True, stop=True)
                        last.then_inc(sem("dn_a_in"), 1)
                    if lat >= 0:
                        for d, st in enumerate(streams):
                            tc = st.tokens(i)
                            if lat >= 1:
                                pe.wait_ge(sem("dn_o"), nth(lat - 1, d))
                            for h in heads:
                                mm(st.head(2, h), sel(d, h), o_g[:, tc], start=True, stop=False)
                                mm(st.head(2, h), ident_b, incl[d], start=False, stop=True)
                            for h in heads:
                                last = mm(st.head(3, h), proj[:, DNK + h, tc], proj[:, DNQ + h, tc], start=True, stop=True)
                            last.then_inc(sem("dn_q_in"), 1)
                        for d, st in enumerate(streams):
                            pe.wait_ge(sem("dn_aexp"), nth(i, d))
                            for h in heads:
                                last = mm(st.head(0, h), sel(d, h), o_eg[:, st.tokens(i)], start=True, stop=True)
                            last.then_inc(sem("dn_q_in"), 1)
                    for d, st in enumerate(streams):
                        pe.wait_ge(sem("dn_level"), nth(i, d, LEVELS))
                        for h in heads:
                            last = tr(st.head(1, h), st.LV[0][:, h, :], ident)
                        last.then_inc(sem("dn_y_in"), 1)
                    for k in range(1, LEVELS):
                        for d, st in enumerate(streams):
                            pe.wait_ge(sem("dn_level"), nth(i, d, LEVELS, k))
                            pe.wait_ge(sem("dn_x"), nth(i, d, LEVELS - 1, k - 1))
                            for h in heads:
                                last = mm(st.head(1, h), st.LV[k][:, h, :], st.X[:, h, :], start=True, stop=True)
                            last.then_inc(sem("dn_y_in"), 1)
                            if k >= 2:
                                if k == 2 and lat >= 0:
                                    pe.wait_ge(sem("dn_q"), nth(lat, d, 2))
                                for h in heads:
                                    last = tr(st.head(3, h), st.X[:, h, :], ident)
                                last.then_inc(sem("dn_t_in"), 1)
                        for d, st in enumerate(streams):
                            pe.wait_ge(sem("dn_y"), nth(i, d, LEVELS - 1, k - 1))
                            pe.wait_ge(sem("dn_xt"), nth(i, d, LEVELS, k - 1))
                            for h in heads:
                                a, b = (st.XT, st.Y) if k < LEVELS - 1 else (st.Y, st.XT)
                                last = mm(st.head(2, h), a[:, h, :], b[:, h, :], start=True, stop=True)
                            last.then_inc(sem("dn_z_in"), 1)
                    for d, st in enumerate(streams):
                        pe.wait_ge(sem("dn_xt"), nth(i, d, LEVELS, LEVELS - 1))
                        pe.wait_ge(sem("dn_scaled"), nth(i, d))
                        for h in heads:
                            last = mm(st.head(1, h), st.KB[:, h, :], st.XT[:, h, :], start=True, stop=True)
                        last.then_inc(sem("dn_w_in"), 1)
                    for d, st in enumerate(streams):
                        pe.wait_ge(sem("dn_w"), nth(i, d))
                        for h in heads:
                            last = mm(st.head(2, h), st.XT[:, h, :], st.VB[:, h, :], start=True, stop=i == 0)
                            if i > 0:
                                last = mm(st.head(2, h), st.WT[:, h, :], st.ST[:, h, :], start=False, stop=True)
                        last.then_inc(sem("dn_u_in"), 1)
                    for d, st in enumerate(streams):
                        pe.wait_ge(sem("dn_u"), nth(i, d))
                        if lat >= 0:
                            pe.wait_ge(sem("dn_q"), nth(lat, d, 2, 1))
                            for h in heads:
                                mm(st.head(3, h), st.ST[:, h, :], st.QG[:, h, :], start=True, stop=False)
                                last = mm(st.head(3, h), st.U[:, h, :], st.ATTN[:, h, :], start=False, stop=True)
                            last.then_inc(sem("dn_o_in"), 1)
                        for h in heads:
                            last = mm(st.head(0, h), st.KDC[:, h, :], st.U[:, h, :], start=True, stop=True)
                        last.then_inc(sem("dn_s_in"), 1)

            def up(layer, c0):
                stage = f"up{layer}"
                h_ready = ready(f"ffn{layer}", 2 if c0 == 0 else 1)

                def body(q, i):
                    which, f = q // 2 % 2, 2 * (q // 4) + q % 2
                    free = sem(f"ffn_act{layer}" if which else f"ffn_silu{layer}")
                    if not isinstance(i, int):
                        pe.wait_ge(free, 4 * i + (f - 1))
                    elif 4 * i + f >= 2:
                        pe.wait_ge(free, 4 * i + f - 1)
                    first = isinstance(i, int) and 8 * i + q == 0
                    split_product(stage, q, i, 4 * which + 2 * (q % 2), c0, h_ready if first else None)
                rounds(stage, body)

            def down(layer, c0):
                stage = f"down{layer}"
                j0, n_loads, _, _ = PLAN[stage]

                def body(k, i):
                    n, half = k // 2, k % 2
                    a = 2 * n
                    if half == 0 and not (isinstance(i, int) and i == 0):
                        pe.wait_ge(sem(f"down_added{layer}"), per * (2 * i + n - 1))
                    pe.wait_ge(sem("w_lo"), 4 * i + (SPLIT[stage] + k + 1))
                    slot_ = (j0 + k) % SLOTS
                    for kk in range(FC // 2):
                        b, w = FC // 2 * half + kk, slice(P * kk, P * kk + P)
                        if b < DOWN_SPLIT:
                            if isinstance(i, int) and i == 0 and n == 0:
                                pe.wait_ge(sem("h_ready"), H_BASE[stage] + b + 1)
                            passes = ((wd_hi[half][:, kk, :], act_hi(b)), (wd_hi[half][:, kk, :], proj_lo[:, b, :]),
                                      (ring_lo_flat[:, slot_, w], act_hi(b)))
                        else:
                            passes = ((ring[:, slot_, w], proj[:, b, :]),)
                        for m, (weight, moving) in enumerate(passes):
                            for lo, hi in segments(c0):
                                last = mm(ps(a, lo - c0, hi - c0), weight, moving[:, lo:hi], start=b == 0 and m == 0,
                                          stop=b == FC - 1 and m == len(passes) - 1)
                    last.then_inc(sem("products"), 1)

                per = 2 if c0 == 0 else 1
                pe.wait_ge(sem(f"ffn_act{layer}"), FC)
                for k in range(4):
                    body(k, 0)
                with pe.Fori(1, n_loads // 4) as i:
                    for k in range(4):
                        body(k, i)

            for layer in range(2):
                tag = f"mix{layer}"
                if layer == 0:
                    pe.wait_ge(sem("x_moved"), 8)
                norm_sums(tag, 0)
                project(f"proj{layer}", 0, ready(tag, 2), f"proj_moved{layer}")
                pe.wait_ge(sem(f"proj_moved{layer}"), 24 if layer == 0 else 22)
                if layer == 0:
                    turn("even")
                    pe.wait_ge(sem("moved_even"), 3 * NT)
                    gates(0)
                    pe.wait_ge(sem("gates_moved0"), 2)
                    rope(0)
                    pe.wait_ge(sem("rope_done0"), 8)
                    attention(0)
                    pe.wait_ge(sem("att_y0"), 24)
                    pe.wait_ge(sem("mod_ready"), 2)
                    row_columns(0, [e_ib])
                    ends(0, 0)
                    ends(0, 1)
                    mlstm()
                    pe.wait_ge(sem("ml_out"), 2 * HEADS)
                    unit_norm_sums(2 * HEADS)
                    pe.wait_ge(sem("y_gated0"), HEADS)
                else:
                    pe.wait_ge(sem("conv_silu"), 12)
                    pe.wait_ge(sem("proj_moved1"), 22)
                    head_norm_sums("l2", lambda i: gates(1, range(i - 4, i - 3)) if i >= 4 else None)
                    pe.wait_ge(sem("hnorm"), HEAD_BASE["l2"] + 8)
                    turn("odd")
                    pe.wait_ge(sem("moved_odd"), 3 * NT)
                    head_norm_sums("qk")
                    pe.wait_ge(sem("hnorm"), HEAD_BASE["qk"] + 5)
                    pe.wait_ge(sem("gates_moved1"), 2)
                    rope(1)
                    pe.wait_ge(sem("keys_spread"), 64)
                    attention(1)
                    pe.wait_ge(sem("att_y1"), 32)
                    row_columns(1, [o_g, o_gb])
                    ends(1, 0)
                    deltanet()
                    pe.wait_ge(sem("dn_state"), 2 * STEPS)
                    pe.wait_ge(sem("dn_o"), 8)
                    head_norm_sums("dn")
                    pe.wait_ge(sem("y_gated1"), HEADS)
                c0 = 0 if layer == 0 else CTX
                project(f"out{layer}", c0, ready(f"out{layer}", 1), f"out_added{layer}", 2 if layer == 0 else 1)
                pe.wait_ge(sem(f"out_added{layer}"), 8 * (2 if c0 == 0 else 1))
                norm_sums(f"ffn{layer}", c0)
                up(layer, c0)
                down(layer, c0)
                pe.wait_ge(sem(f"down_added{layer}"), 8 * (2 if c0 == 0 else 1))
            norm_sums("final", CTX)
            for i in range(8):
                t, half = divmod(i, 2)
                pe.wait_ge(sem("final_normed"), 8)
                if i >= 2:
                    pe.wait_ge(sem("out_moved"), i - 1)
                for k in range(4):
                    last = tr(ps(2 + i % 2, P * k, P * k + P), hT[:, 4 * half + k, CTX + P * t:CTX + P * t + P], ident)
                last.then_inc(sem("out_turned"), 1)

        @block.scalar
        def _(act):
            step_no = [0]

            def A(out_, in_, f, **kw):
                return nc.scalar.activation(out_, in_, f, **kw)

            def then(ins):
                step_no[0] += 1
                ins.then_inc(sem("act_step"), 1)
                act.wait_ge(sem("act_step"), step_no[0])

            act.wait_ge(sem("vec_moved"), 2)
            A(silu_c[:].rearrange("p k s -> p s k"), vec_b[:, V_C:V_C + 16].rearrange("p (s k) -> p s k", s=2), ACT.Silu).then_inc(sem("silu_c"), 1)
            for k in range(0, KD):
                act.wait_ge(sem("x_turned"), k + 1)
                A(xT[:, k, :], ps(2 + 2 * (k % 2), 0, T), ACT.Copy).then_inc(sem("x_moved"), 1)
            act.wait_ge(sem("lam_sums"), 1)
            A(small[:, 2:4], small[:, 0:2], ACT.Exp).then_inc(sem("lam_exp"), 1)
            act.wait_ge(sem("gates_in"), 16 * 11)
            act.wait_ge(sem("vec_moved"), 2)
            A(gate_b[:, 4:5], gate_b[:, 3:4], ACT.Exp).then_inc(sem("lam_exp"), 1)
            A(small[:, 4:5], vec_b[:, G_DA:G_DA + 1], ACT.Copy, scale=1.0 - LAM_INIT).then_inc(sem("lam_exp"), 1)

            norm_no = [0]

            def high_part(stage, q, i=0):
                j0, _, _, _ = PLAN[stage]
                k, half = q // 2, q % 2
                slot_ = (j0 + k) % SLOTS
                if half == 0:
                    act.wait_ge(sem(f"weights_in{slot_}"), 16 * i + 16 * ((j0 + k) // SLOTS + 1))
                raw = ring[:, slot_, :].rearrange("p (k n) -> p k n", k=KD)[:, :, P * half:P * half + P]
                A(w_hi[half][:], raw, ACT.Copy).then_inc(sem("w_hi"), 1)

            def high_parts(stage, between=None):
                _, n, _, done = PLAN[stage]

                def body(p, i, more=True):
                    act.wait_ge(sem("products"), 8 * i + (done + p + 1))
                    if more:
                        high_part(stage, p + 2, i)
                    if between is not None:
                        between(p, i)

                full = (2 * n - 2) // 8
                for p in range(8 * min(full, 1)):
                    body(p, 0)
                if full > 1:
                    with act.Fori(1, full) as i:
                        for p in range(8):
                            body(p, i)
                for p in range(2 * n - 8 * full):
                    if 8 * full + p + 2 < 2 * n or between is not None:
                        body(p, full, 8 * full + p + 2 < 2 * n)

            def conv_silus():
                _, n, _, done = PLAN["proj1"]
                lag = 2
                for p in range(max(2 * n, DNQ + 12 + lag)):
                    if p + 2 < 2 * n:
                        act.wait_ge(sem("products"), done + p + 1)
                        high_part("proj1", (p + 2) % 8, (p + 2) // 8)
                    b = p - lag - DNQ
                    if 0 <= b < 12:
                        act.wait_ge(sem("conv_sum"), b + 1)
                        A(proj[:, DNQ + b, :], sq[:, b % 2, :], ACT.Silu).then_inc(sem("conv_silu"), 1)

            def down(layer, c0):
                stage = f"down{layer}"
                j0, n, _, done = PLAN[stage]

                def weights_high(q, i=0):
                    slot_, w = (j0 + q) % SLOTS, wd_hi[q % 2]
                    act.wait_ge(sem(f"weights_in{slot_}"), 16 * i + 16 * ((j0 + q) // SLOTS + 1))
                    A(w[:].rearrange("p k n -> p (k n)"), ring[:, slot_, 0:P * w.shape[1]], ACT.Copy).then_inc(sem("w_hi"), 1)

                act.wait_ge(sem("products"), done)
                weights_high(0)
                for k in range(DOWN_SPLIT):
                    if k == FC // 2:
                        weights_high(1)
                    act.wait_ge(sem(f"ffn_act{layer}"), k + 1)
                    A(act_hi(k)[:, c0:T], proj[:, k, c0:T], ACT.Copy).then_inc(sem("h_hi"), 1)
                full = (n - 2) // 4
                with act.Fori(0, full) as i:
                    for p in range(4):
                        act.wait_ge(sem("products"), 4 * i + (done + p + 1))
                        weights_high(p + 2, i)
                for p in range(n - 2 - 4 * full):
                    act.wait_ge(sem("products"), 4 * full + done + p + 1)
                    weights_high(p + 2, full)

            def split_y(layer, c0):
                high_part(f"out{layer}", 0)
                for k in range(KD):
                    if k >= 4:
                        act.wait_ge(sem(f"y_gated{layer}"), k - 3)
                    A(h_hi[:, k, c0:T], hT[:, k, c0:T], ACT.Copy).then_inc(sem("h_hi"), 1)
                high_part(f"out{layer}", 1)
                high_parts(f"out{layer}")

            def norm(tag, c0, shift):
                n = norm_no[0]
                for k in range(KD):
                    if n or k >= 2:
                        act.wait_ge(sem("squares_summed"), max(n * KD + k - 1, n * KD))
                    if k == 0:
                        act.wait_ge(sem("x_moved"), 8)
                    A(sq[:, k % 2, c0:T], xT[:, k, c0:T], ACT.Square).then_inc(sem("squared"), 1)
                act.wait_ge(sem("mean_square"), n + 1)
                A(rs[:, 0, c0:T], rs[:, 1, c0:T], ACT.Sqrt).then_inc(sem("root"), 1)
                norm_no[0] += 1
                if shift is None:
                    return
                layer, at = shift
                stage = ("proj" if at == SH1 else "up") + str(layer)
                high_part(stage, 0)
                parts = [(CTX, T, 0)] + ([(0, CTX, 1)] if c0 == 0 else [])
                m = 0
                for k in range(KD):
                    for lo, hi, s in parts:
                        m += 1
                        act.wait_ge(sem("h_scaled"), SCALED_BASE[tag] + m)
                        A(h_hi[:, k, lo:hi], hT[:, k, lo:hi], ACT.Identity, bias=modT[:, layer, at + k, s:s + 1]).then_inc(sem("h_hi"), 1)
                high_part(stage, 1)

            def move(stage):
                for i, (srcs, dst) in enumerate(transposes(stage)):
                    act.wait_ge(sem(f"turned_{stage}"), i + 1)
                    A(dst, ps(i % 4, 0, P * len(srcs)), ACT.Copy).then_inc(sem(f"moved_{stage}"), 1)

            def head_norm(stage):
                items = head_norm_items(stage)
                for i in range(len(items) + 1):
                    if i < len(items):
                        src, _, _, _, _, n = items[i]
                        if i >= 2:
                            act.wait_ge(sem("hsum"), HEAD_BASE[stage] + i - 1)
                        A(sq[:, i % 2, 0:n], src, ACT.Square).then_inc(sem("hsq"), 1)
                    if i >= 1:
                        n = items[i - 1][5]
                        act.wait_ge(sem("hms"), HEAD_BASE[stage] + i)
                        A(rs[:, (i - 1) % 2, 0:n], rs[:, (i - 1) % 2, 0:n], ACT.Sqrt).then_inc(sem("hroot"), 1)

            def unit_norm(u):
                if u not in UNIT_NORM:
                    return
                stage, i = UNIT_NORM[u]
                act.wait_ge(sem("att_y0"), 24)
                if stage == "ml":
                    act.wait_ge(sem("ml_out"), u)
                A(sq[:, 1, :], head_norm_items(stage)[i][0], ACT.Square).then_inc(sem("hsq"), 1)
                act.wait_ge(sem("hms"), HEAD_BASE[stage] + i + 1)
                A(rs[:, 0, :], rs[:, 0, :], ACT.Sqrt).then_inc(sem("hroot"), 1)

            def attention(layer):
                a = Att(layer)
                n = len(a.tiles)

                def exps(i):
                    for m in range(a.maps):
                        g = i * a.maps + m
                        act.wait_ge(sem(f"att_max{layer}"), g + 1)
                        if i >= 2:
                            act.wait_ge(sem(f"att_turned{layer}"), i - 1)
                        nk = a.keys(i)
                        b = 2 * m if a.maps == 2 else 2 * (i % 2)
                        o = 8 * (i % 2)
                        A(a.E[i % 2][m][:, 0:nk], ps(b, 0, nk), ACT.Exp, bias=small[:, 8 + o + m:9 + o + m], scale=64 ** -0.5,
                          accum_out=small[:, 10 + o + m:11 + o + m]).then_inc(sem(f"att_exp{layer}"), 1)

                exps(0)
                for i in range(n):
                    if i + 1 < n:
                        exps(i + 1)
                    act.wait_ge(sem(f"att_turned{layer}"), i + 1)
                    if i >= 2:
                        act.wait_ge(sem(f"att_out{layer}"), i - 1)
                    nk = a.keys(i)
                    A(a.PT[i % 2][:, 0:nk], ps(4, 0, nk), ACT.Copy).then_inc(sem(f"att_pt{layer}"), 1)

            def soft_rows(layer):
                if layer == 0:
                    act.wait_ge(sem("rows_in0"), 1)
                    then(A(e_t, rowF, ACT.Abs))
                    then(A(e_t, e_t, ACT.Exp, scale=-1.0))
                    A(e_t, e_t, ACT.Ln, bias=1.0).then_inc(sem("soft0"), 1)
                    act.wait_ge(sem("rows_diff0"), 1)
                    A(e_inter, e_inter, ACT.Exp)
                    A(e_em, e_m, ACT.Exp, scale=-1.0)
                    A(endr[:, 4, 0:NT], endr[:, 4, 0:NT], ACT.Exp).then_inc(sem("rows_exp0"), 1)
                else:
                    act.wait_ge(sem("rows_in1"), 1)
                    for k, row in enumerate((o_rowI, o_rowF)):
                        dst = (o_gb, o_t)[k]
                        then(A(dst, row, ACT.Abs))
                        then(A(dst, dst, ACT.Exp, scale=-1.0))
                        A(dst, dst, ACT.Ln, bias=1.0).then_inc(sem("soft1"), 1)
                    act.wait_ge(sem("rows_diff1"), 1)
                    A(o_eg, o_g, ACT.Exp).then_inc(sem("rows_exp1"), 1)

            def mlstm():
                act.wait_ge(sem("ml_wexp"), 2)
                A(cols[:, 1], cols[:, 1], ACT.Exp).then_inc(sem("ml_ready"), 1)
                act.wait_ge(sem("ml_ready"), 1)
                for u in range(2 * HEADS):
                    d, h = divmod(u, HEADS)
                    r = u
                    if u >= 1:
                        act.wait_ge(sem("ml_u"), 5 * u)
                    for ch in range(NT):
                        A(kw[:, ch, :], tok_e[:, ch, 1024 + 64 * h:1088 + 64 * h], ACT.Copy, scale=cols[:, 1, ch, r:r + 1]).then_inc(sem("ml_kw"), 1)
                    act.wait_ge(sem("ml_pe"), 6 * u + 1)
                    for ch in range(NT):
                        last = A(pexp[:, P * ch:P * ch + P], ps(0, P * ch, P * ch + P), ACT.Exp, bias=cols[:, 0, ch, r:r + 1])
                    last.then_inc(sem("ml_exp"), 1)
                    unit_norm(u)
                    act.wait_ge(sem("ml_pe"), 6 * u + 5)
                    if u >= 1:
                        act.wait_ge(sem("ml_out"), u)
                    A(den, ps(0, 0, T), ACT.Abs).then_inc(sem("ml_den"), 1)

            def deltanet():
                act.wait_ge(sem("dn_wexp"), 2)
                A(cols[:, 0:3], cols[:, 0:3], ACT.Exp)
                A(endb[:], endb[:], ACT.Exp).then_inc(sem("dn_cols"), 1)
                streams = [Stream(d) for d in range(2)]
                act.wait_ge(sem("dn_cols"), 1)

                def exps(dst, st, b, i):
                    for h in range(HEADS):
                        r = 4 * st.d + h
                        last = A(dst[:, h, :], st.head(b, h), ACT.Exp, bias=cols[:, 3, st.chunk(i), r:r + 1])
                    return last

                for i in range(STEPS):
                    lat = i - LAT_STEP
                    for d, st in enumerate(streams):
                        act.wait_ge(sem("dn_a_in"), nth(i, d))
                        exps(st.X, st, 0, i).then_inc(sem("dn_aexp"), 1)
                    if lat >= 0:
                        for d, st in enumerate(streams):
                            act.wait_ge(sem("dn_q_in"), nth(lat, d, 2))
                            exps(st.Y, st, 2, i).then_inc(sem("dn_qexp"), 1)
                    for k in range(1, LEVELS):
                        for d, st in enumerate(streams):
                            if k == 1 and lat >= 0:
                                act.wait_ge(sem("dn_q"), nth(lat, d, 2))
                            act.wait_ge(sem("dn_y_in"), nth(i, d, LEVELS, k))
                            if k >= 2:
                                act.wait_ge(sem("dn_z_in"), nth(i, d, LEVELS - 1, k - 2))
                            A(st.Y, st.ps(1), ACT.Copy).then_inc(sem("dn_y"), 1)
                    for d, st in enumerate(streams):
                        act.wait_ge(sem("dn_w_in"), nth(i, d))
                        A(st.WT, st.ps(1), ACT.Copy, scale=-1.0).then_inc(sem("dn_w"), 1)

            def gate_values(layer, first, c0, stage):
                for h in range(HEADS):
                    A(proj[:, first + h, c0:T], proj[:, first + h, c0:T], ACT.Sigmoid if layer == 0 else ACT.Silu).then_inc(sem(f"out_gate{layer}"), 1)

            def up(layer, c0):
                w = T - c0

                def silu(p, i):
                    if p % 4 >= 2:
                        return
                    f = 2 * (p // 4) + p % 4
                    if not isinstance(i, int):
                        act.wait_ge(sem(f"ffn_act{layer}"), 4 * i + (f - 1))
                    elif 4 * i + f >= 2:
                        act.wait_ge(sem(f"ffn_act{layer}"), 4 * i + f - 1)
                    A(sq[:, f % 2, 0:w], ps(2 * (f % 2), 0, w), ACT.Silu).then_inc(sem(f"ffn_silu{layer}"), 1)

                high_parts(f"up{layer}", silu)

            for layer in range(2):
                c0 = 0 if layer == 0 else CTX
                act.wait_ge(sem("mod_ready"), layer + 1)
                norm(f"mix{layer}", 0, (layer, SH1))
                if layer == 0:
                    high_parts("proj0")
                    act.wait_ge(sem("h_back"), KD)
                    move("even")
                    attention(0)
                    soft_rows(0)
                    mlstm()
                    gate_values(0, MLO, 0, "ml")
                    unit_norm(2 * HEADS)
                else:
                    conv_silus()
                    act.wait_ge(sem("proj_moved1"), 22)
                    gate_values(1, DNZ, CTX, "dn")
                    act.wait_ge(sem("conv_silu"), 12)
                    head_norm("l2")
                    act.wait_ge(sem("h_back"), 2 * KD)
                    move("odd")
                    head_norm("qk")
                    attention(1)
                    soft_rows(1)
                    deltanet()
                    act.wait_ge(sem("dn_o"), 8)
                    head_norm("dn")
                split_y(layer, c0)
                act.wait_ge(sem(f"out_added{layer}"), 8 * (2 if c0 == 0 else 1))
                norm(f"ffn{layer}", c0, (layer, SH2))
                up(layer, c0)
                down(layer, c0)
                act.wait_ge(sem(f"down_added{layer}"), 8 * (2 if c0 == 0 else 1))
            norm("final", CTX, None)
            for i in range(8):
                t, half = divmod(i, 2)
                act.wait_ge(sem("out_turned"), i + 1)
                A(out_tok[:, t, 512 * half:512 * half + 512], ps(2 + i % 2, 0, 512), ACT.Copy).then_inc(sem("out_moved"), 1)

        @block.vector
        def _(dve):
            V = nc.vector
            step_no = [0]

            def then(ins):
                step_no[0] += 1
                ins.then_inc(sem("dve_step"), 1)
                dve.wait_ge(sem("dve_step"), step_no[0])

            dve.wait_ge(sem("vec_turned"), 2)
            V.tensor_copy(vec_a[:], ps(0, 0, 96)).then_inc(sem("vec_moved"), 1)
            V.tensor_copy(vec_b[:], ps(1, 0, NVEC)).then_inc(sem("vec_moved"), 1)
            dve.wait_ge(sem("gates_in"), 16 * 11)
            lam2 = lam_in.rearrange("p (a b) n -> p a b n", b=2)
            then(V.tensor_tensor(lam_tmp, lam2[:, :, 0, :], lam2[:, :, 1, :], ALU.mult))
            V.tensor_reduce(small[:, 0:2], lam_tmp, AX_X, ALU.add).then_inc(sem("lam_sums"), 1)
            dve.wait_ge(sem("lam_exp"), 2)
            then(V.tensor_tensor(small[:, 5:6], small[:, 3:4], small[:, 2:3], ALU.subtract))
            then(V.tensor_scalar(small[:, 6:7], small[:, 5:6], LAM_INIT, None, ALU.subtract))
            then(V.tensor_scalar(gate_b[:, 5:6], gate_b[:, 4:5], -1.0, None, ALU.mult))
            dve.wait_ge(sem("vec_moved"), 2)
            mod_flat = modT[:].rearrange("p l n s -> p (l n) s")

            def modulation(lo, hi, scales):
                then(V.tensor_tensor(mod_flat[:, lo:hi], PS[:, 6 * BANK + ADA_COLS + 2 * lo:6 * BANK + ADA_COLS + 2 * hi].rearrange("p (n s) -> p n s", s=2),
                                     vec_a[:, lo:hi].unsqueeze(2).to_broadcast([P, hi - lo, 2]), ALU.add))
                for l, j in scales:
                    at = (SC1, SC2)[j]
                    g = vec_b[:, (G_MIX, G_FFN)[j] + 8 * l:(G_MIX, G_FFN)[j] + 8 * l + 8]
                    last = V.scalar_tensor_tensor(out=gmT[:, l, j], in0=modT[:, l, at:at + 8, :], scalar=1.0,
                                                  in1=g.unsqueeze(2).to_broadcast([P, KD, 2]), op0=ALU.add, op1=ALU.mult)
                last.then_inc(sem("mod_ready"), 1)

            def ada_rows(n):
                dve.wait_ge(sem("products"), 2 * n + 2 if n < 8 else PLAN["adb0"][3] + 2 * (n - 8) + 2)
                if n >= 2:
                    dve.wait_ge(sem("ada_turned"), n - 1)
                b = n % 2 if n < 8 else 6
                V.tensor_copy(ada_row(n), PS[0:2, b * BANK:b * BANK + 256]).then_inc(sem("ada_rows"), 1)

            for n in range(8):
                ada_rows(n)
            dve.wait_ge(sem("ada_turned"), 8)
            modulation(0, 16, [(0, 0)])

            norm_no = [0]

            def norm(tag, c0, gains, shift, last_gain=None):
                n = norm_no[0]
                dve.wait_ge(sem("squares_summed"), KD * (n + 1))
                V.tensor_scalar(rs[:, 1, c0:T], PS[:, 0:T - c0], 1.0 / D, EPS, ALU.mult, ALU.add).then_inc(sem("mean_square"), 1)
                dve.wait_ge(sem("root"), n + 1)
                then(V.reciprocal(rs[:, 1, c0:T], rs[:, 0, c0:T]))
                norm_no[0] += 1
                parts = [(CTX, T, 0)] + ([(0, CTX, 1)] if c0 == 0 else [])

                def low_part(k):
                    for j, (lo, hi, s) in enumerate(parts):
                        dve.wait_ge(sem("h_hi"), H_BASE[tag] + len(parts) * k + j + 1)
                        V.scalar_tensor_tensor(out=hT_lo[:, k, lo:hi], in0=hT[:, k, lo:hi], scalar=shift[:, k, s:s + 1],
                                               in1=h_hi[:, k, lo:hi], op0=ALU.add, op1=ALU.subtract).then_inc(sem("h_ready"), 1)

                for k in range(KD):
                    if gains is not None and k >= 1:
                        low_part(k - 1)
                    for lo, hi, s in parts:
                        g = gains[:, k, s:s + 1] if gains is not None else last_gain[:, k:k + 1]
                        V.scalar_tensor_tensor(out=hT[:, k, lo:hi], in0=xT[:, k, lo:hi], scalar=g, in1=rs[:, 1, lo:hi],
                                               op0=ALU.mult, op1=ALU.mult).then_inc(sem("h_scaled" if gains is not None else "final_normed"), 1)
                if gains is not None:
                    low_part(KD - 1)

            def project_out(layer):
                n = 24 if layer == 0 else 22
                _, _, _, done = PLAN[f"proj{layer}"]
                if layer == 1:
                    for b in range(n):
                        dve.wait_ge(sem("products"), done + b + 1)
                        V.tensor_scalar(proj[:, b, :], ps(2 * (b % 4), 0, T), 1.0, None, ALU.mult).then_inc(sem("proj_moved1"), 1)
                        if DNQ <= b < DNQ + 12:
                            dve.wait_ge(sem("proj_moved1"), b + 1)
                            conv(b - DNQ)
                    return
                with dve.Fori(0, n // 8) as i:
                    for b in range(8):
                        dve.wait_ge(sem("products"), 8 * i + (done + b + 1))
                        V.tensor_scalar(proj[:, bass.ds(8 * i + b, 1), :].rearrange("p a t -> p (a t)"), ps(2 * (b % 4), 0, T), 1.0, None,
                                        ALU.mult).then_inc(sem("proj_moved0"), 1)

            def add_in(k, b, layer, ga, c0, signal):
                parts = [(CTX, T, 0)] + ([(0, CTX, 1)] if c0 == 0 else [])
                for lo, hi, s in parts:
                    xs = xT[:, bass.ds(k, 1), lo:hi].rearrange("p a t -> p (a t)")
                    g = modT[:, layer, bass.ds(ga + k, 1), s:s + 1].rearrange("p a t -> p (a t)")
                    V.scalar_tensor_tensor(out=xs, in0=ps(b, lo - c0, hi - c0), scalar=g, in1=xs, op0=ALU.mult, op1=ALU.add).then_inc(sem(signal), 1)

            def head_norm(stage):
                items = head_norm_items(stage)
                for i in range(len(items) + 1):
                    if i < len(items):
                        _, _, scale, _, _, n = items[i]
                        dve.wait_ge(sem("hsum"), HEAD_BASE[stage] + i + 1)
                        if i >= 2:
                            dve.wait_ge(sem("hnorm"), HEAD_BASE[stage] + i - 1)
                        V.tensor_scalar(rs[:, i % 2, 0:n], ps(2 * (i % 2), 0, n), scale, EPS, ALU.mult, ALU.add).then_inc(sem("hms"), 1)
                    if i >= 1:
                        src, _, _, gain, dst, n = items[i - 1]
                        r = rs[:, (i - 1) % 2, 0:n]
                        dve.wait_ge(sem("hroot"), HEAD_BASE[stage] + i)
                        then(V.reciprocal(r, r))
                        V.scalar_tensor_tensor(out=dst, in0=src, scalar=gain, in1=r, op0=ALU.mult, op1=ALU.mult).then_inc(sem("hnorm"), 1)

            def unit_norm(u):
                if u not in UNIT_NORM:
                    return
                stage, i = UNIT_NORM[u]
                src, _, scale, gain, dst, _ = head_norm_items(stage)[i]
                r = rs[:, 0, :]
                dve.wait_ge(sem("hsum"), HEAD_BASE[stage] + i + 1)
                if i >= 1 or stage == "ml":
                    dve.wait_ge(sem("hnorm"), HEAD_BASE[stage] + i)
                V.tensor_scalar(r, ps(6, 0, T), scale, EPS, ALU.mult, ALU.add).then_inc(sem("hms"), 1)
                dve.wait_ge(sem("hroot"), HEAD_BASE[stage] + i + 1)
                then(V.reciprocal(r, r))
                if stage == "ml":
                    dve.wait_ge(sem("ml_out"), u)
                V.scalar_tensor_tensor(out=dst, in0=src, scalar=gain, in1=r, op0=ALU.mult, op1=ALU.mult).then_inc(sem("hnorm"), 1)

            def rope(layer):
                t1, t2 = rs[:, 0, 0:LAT], rs[:, 1, 0:LAT]
                cos, sin = rot_at[layer][:, 0:LAT], rot_at[layer][:, LAT:2 * LAT]
                dve.wait_ge(sem("rotary_in"), 16 * (layer + 1))
                for i, b in enumerate(ROPE[layer]):
                    xs = proj[:, b, CTX:T]
                    dve.wait_ge(sem(f"rope_swapped{layer}"), i + 1)
                    if i >= 1:
                        dve.wait_ge(sem(f"rope_done{layer}"), i)
                    V.tensor_tensor(t1, xs, cos, ALU.mult).then_inc(sem("rope_parts"), 1)
                    V.tensor_tensor(t2, ps(4 + i % 2, 0, LAT), sin, ALU.mult).then_inc(sem("rope_parts"), 1)
                    rope_no[0] += 2
                    dve.wait_ge(sem("rope_parts"), rope_no[0])
                    V.tensor_tensor(xs, t1, t2, ALU.add).then_inc(sem(f"rope_done{layer}"), 1)

            rope_no = [0]

            def gate_rows(layer):
                rows = (rowI, rowF) if layer == 0 else (o_rowI, o_rowF)
                for kind in range(2):
                    dve.wait_ge(sem("gate_rows"), 2 * layer + kind + 1)
                    src = PS[0:GROW, (4 + 2 * kind) * BANK:(4 + 2 * kind) * BANK + T]
                    if layer == 0:
                        ins = V.tensor_scalar(rows[kind], src, gate_b[:, kind:kind + 1], None, ALU.add)
                    elif kind == 0:
                        ins = V.tensor_copy(rows[kind], src)
                    else:
                        ins = V.tensor_scalar(rows[kind], src, gate_b[:, 2:3], None, ALU.add)
                    ins.then_inc(sem(f"gates_moved{layer}"), 1)

            def attention(layer):
                a = Att(layer)
                n = len(a.tiles)

                def maxima(i):
                    o = 8 * (i % 2)
                    for m in range(a.maps):
                        g = i * a.maps + m
                        b = 2 * m if a.maps == 2 else 2 * (i % 2)
                        dve.wait_ge(sem(f"att_scores{layer}"), g + 1)
                        then(V.tensor_reduce(small[:, 12 + o + m:13 + o + m], ps(b, 0, a.keys(i)), AX_X, ALU.max))
                        V.tensor_scalar(small[:, 8 + o + m:9 + o + m], small[:, 12 + o + m:13 + o + m], -(64 ** -0.5), None,
                                        ALU.mult).then_inc(sem(f"att_max{layer}"), 1)

                maxima(0)
                for i in range(n):
                    o = 8 * (i % 2)
                    nk = a.keys(i)
                    e = [a.E[i % 2][m][:, 0:nk] for m in range(a.maps)]
                    dve.wait_ge(sem(f"att_exp{layer}"), a.maps * (i + 1))
                    then(V.reciprocal(small[:, 12 + o:12 + o + a.maps], small[:, 10 + o:10 + o + a.maps]))
                    if a.maps == 2:
                        then(V.tensor_tensor(small[:, 14 + o:15 + o], small[:, 13 + o:14 + o], small[:, 6:7], ALU.mult))
                        then(V.tensor_scalar(e[0], e[0], small[:, 12 + o:13 + o], None, ALU.mult))
                        V.scalar_tensor_tensor(out=e[0], in0=e[1], scalar=small[:, 14 + o:15 + o], in1=e[0], op0=ALU.mult,
                                               op1=ALU.add).then_inc(sem(f"att_probs{layer}"), 1)
                    else:
                        V.tensor_scalar(e[0], e[0], small[:, 12 + o:13 + o], None, ALU.mult).then_inc(sem(f"att_probs{layer}"), 1)
                    if i + 1 < n:
                        maxima(i + 1)
                    if i >= 1:
                        output(i - 1)
                    if layer == 0 and i < 20:
                        ada_rows(8 + 2 * i)
                        ada_rows(9 + 2 * i)
                output(n - 1)

            def att_output(layer):
                a = Att(layer)

                def go(i):
                    dve.wait_ge(sem(f"att_out{layer}"), i + 1)
                    lo, hi = a.rows(i)
                    V.tensor_copy(a.y(i), PS[lo:hi, 7 * BANK:7 * BANK + P]).then_inc(sem(f"att_y{layer}"), 1)
                return go

            def ends_of(row, dst):
                v = row.rearrange("p (c n) -> p c n", n=P)
                then(V.tensor_copy(dst[0:32, 0:NT], v[0:32, :, P - 1]))
                then(V.tensor_copy(dst[32:GROW, 0:NT], v[32:GROW, :, 0]))

            def spread_ends(layer, w, row):
                if w:
                    dve.wait_ge(sem(f"ends_out{layer}"), w)
                V.tensor_tensor(endx[:], ident[0:GROW, 0:GROW].unsqueeze(1).to_broadcast([GROW, NT, GROW]),
                                row.unsqueeze(2).to_broadcast([GROW, NT, GROW]), ALU.mult).then_inc(sem(f"ends_spread{layer}"), 1)

            def turned(b, s):
                return PS[:, b * BANK:b * BANK + NT * GROW].rearrange("p (c r) -> p c r", c=NT)[:, :, s]

            def bykey(f):
                for d in range(2):
                    f(slice(4 * d, 4 * d + 4), slice(32 * d, 32 * d + 4))

            def rows_even():
                dve.wait_ge(sem("gates_moved0"), 2)
                dve.wait_ge(sem("att_y0"), 24)
                dve.wait_ge(sem("att_out0"), 24)
                V.memset(small[:, 7:8], 0.0).then_inc(sem("rows_in0"), 1)
                dve.wait_ge(sem("soft0"), 1)
                then(V.scalar_tensor_tensor(out=e_logf, in0=rowF, scalar=0.0, in1=e_t, op0=ALU.min, op1=ALU.subtract))
                then(V.tensor_tensor_scan(e_m[0:32], e_logf[0:32], rowI[0:32], 0.0, ALU.add, ALU.max))
                r = slice(32, GROW)
                then(V.tensor_tensor_scan(e_m[r, 0:CTX][:, ::-1], e_logf[r, 0:CTX][:, ::-1], rowI[r, 0:CTX][:, ::-1], 0.0, ALU.add, ALU.max))
                then(V.tensor_tensor_scan(e_m[r, CTX:T][:, ::-1], e_logf[r, CTX:T][:, ::-1], rowI[r, CTX:T][:, ::-1], e_m[r, 0:1], ALU.add, ALU.max))
                then(V.tensor_copy(e_t.rearrange("p (c n) -> p c n", n=P), resets))
                then(V.tensor_tensor_scan(e_b[0:32], e_t[0:32], e_logf[0:32], 0.0, ALU.mult, ALU.add))
                then(V.tensor_tensor_scan(e_b[r][:, ::-1], e_t[r][:, ::-1], e_logf[r][:, ::-1], 0.0, ALU.mult, ALU.add))
                ends_of(e_m, endr[:, 0])
                ends_of(e_b, endr[:, 1])
                then(V.memset(endr[:, 2, :], 0.0))
                then(V.tensor_copy(endr[0:32, 2, 1:NT], endr[0:32, 0, 0:NT - 1]))
                then(V.tensor_copy(endr[r, 2, 0:1], endr[r, 0, 1:2]))
                then(V.tensor_copy(endr[r, 2, NT - 1:NT], endr[r, 0, 0:1]))
                then(V.tensor_copy(endr[r, 2, 2:NT - 1], endr[r, 0, 3:NT]))
                then(V.tensor_tensor(e_ib, rowI, e_b, ALU.subtract))
                then(V.tensor_tensor(e_A, e_b, e_m, ALU.subtract))
                m0 = endr[:, 2, 0:NT].unsqueeze(2).to_broadcast([GROW, NT, P])
                then(V.tensor_tensor(e_inter.rearrange("p (c n) -> p c n", n=P), e_A.rearrange("p (c n) -> p c n", n=P), m0, ALU.add))
                then(V.tensor_tensor(endr[:, 3, 0:NT], endr[:, 1, 0:NT], endr[:, 0, 0:NT], ALU.subtract))
                V.tensor_tensor(endr[:, 4, 0:NT], endr[:, 3, 0:NT], endr[:, 2, 0:NT], ALU.add).then_inc(sem("rows_diff0"), 1)
                dve.wait_ge(sem("rows_exp0"), 1)
                V.memset(small[:, 7:8], 0.0).then_inc(sem("rows_ready0"), 1)
                spread_ends(0, 0, endr[:, 3, 0:NT])
                spread_ends(0, 1, endr[:, 4, 0:NT])
                dve.wait_ge(sem("columns_turned0"), 1)
                bykey(lambda d, s: then(V.tensor_copy(cols[:, 0, :, d], turned(0, s))))
                dve.wait_ge(sem("ends_out0"), 2)
                bykey(lambda d, s: then(V.tensor_copy(endb[:, :, d], turned(3, s))))
                bykey(lambda d, s: V.tensor_tensor(cols[:, 1, :, d], cols[:, 0, :, d], turned(2, s), ALU.add).then_inc(sem("ml_wexp"), 1))
                dve.wait_ge(sem("ml_ready"), 1)

            def mlstm():
                for u in range(2 * HEADS):
                    d, h = divmod(u, HEADS)
                    r = 64 * (h % 2)
                    dve.wait_ge(sem("ml_pe"), 6 * u + 2)
                    V.scalar_tensor_tensor(out=qt[r:r + 64, :], in0=proj[r:r + 64, MLQ + h // 2, :], scalar=64 ** -0.5,
                                           in1=PS[r:r + 64, 4 * BANK:4 * BANK + T], op0=ALU.mult, op1=ALU.mult).then_inc(sem("ml_qt"), 1)
                    for i in range(5):
                        ch, nxt = ORDER[d][i], ORDER[d][i + 1]
                        dve.wait_ge(sem("ml_u"), 5 * u + i + 1)
                        src = PS[r:r + 64, (6 + i % 2) * BANK:(6 + i % 2) * BANK + 256]
                        if i == 0:
                            V.tensor_copy(cst[r:r + 64, nxt, :], src).then_inc(sem("ml_state"), 1)
                        else:
                            dve.wait_ge(sem("ml_state"), 5 * u + i)
                            V.scalar_tensor_tensor(out=cst[r:r + 64, nxt, :], in0=cst[r:r + 64, ch, :], scalar=endb[r:r + 64, ch, u:u + 1],
                                                   in1=src, op0=ALU.mult, op1=ALU.add).then_inc(sem("ml_state"), 1)
                    dve.wait_ge(sem("ml_pe"), 6 * u + 3)
                    dve.wait_ge(sem("ml_exp"), u + 1)
                    V.scalar_tensor_tensor(out=pm, in0=pexp, scalar=64 ** -0.5, in1=ps(2, 0, T), op0=ALU.mult, op1=ALU.mult).then_inc(sem("ml_probs"), 1)
                    unit_norm(u)
                    dve.wait_ge(sem("ml_den"), u + 1)
                    dve.wait_ge(sem("ml_pe"), 6 * u + 6)
                    V.tensor_tensor(den, den, ps(4, 0, T), ALU.max).then_inc(sem("ml_em_read"), 1)
                    dve.wait_ge(sem("ml_em_read"), u + 1)
                    then(V.reciprocal(den, den))
                    y = hT[:, 4 + h, :]
                    if d == 0:
                        V.tensor_tensor(y, den, ps(2, 0, T), ALU.mult).then_inc(sem("ml_out"), 1)
                    else:
                        then(V.tensor_tensor(den, den, ps(2, 0, T), ALU.mult))
                        V.tensor_tensor(y, y, den, ALU.add).then_inc(sem("ml_out"), 1)

            def conv(b):
                acc = sq[:, b % 2, :]
                src = proj[:, DNQ + b, :]
                w = [vec_b[:, CONV + 12 * tap + b:CONV + 12 * tap + b + 1] for tap in range(3)]
                if b >= 2:
                    dve.wait_ge(sem("conv_silu"), b - 1)
                then(V.tensor_scalar(acc, src, w[1], None, ALU.mult))
                for lo, hi in ((0, CTX), (CTX, T)):
                    then(V.scalar_tensor_tensor(out=acc[:, lo + 1:hi], in0=src[:, lo:hi - 1], scalar=w[0], in1=acc[:, lo + 1:hi],
                                                op0=ALU.mult, op1=ALU.add))
                for lo, hi in ((0, CTX), (CTX, T)):
                    ins = V.scalar_tensor_tensor(out=acc[:, lo:hi - 1], in0=src[:, lo + 1:hi], scalar=w[2], in1=acc[:, lo:hi - 1],
                                                 op0=ALU.mult, op1=ALU.add)
                    if lo == 0:
                        then(ins)
                ins.then_inc(sem("conv_sum"), 1)

            def rows_odd():
                dve.wait_ge(sem("gates_moved1"), 2)
                dve.wait_ge(sem("att_y1"), 32)
                V.memset(small[:, 7:8], 0.0).then_inc(sem("rows_in1"), 1)
                dve.wait_ge(sem("soft1"), 2)
                r = slice(32, GROW)
                then(V.scalar_tensor_tensor(out=o_gb, in0=o_rowI, scalar=0.0, in1=o_gb, op0=ALU.min, op1=ALU.subtract))
                then(V.scalar_tensor_tensor(out=o_t, in0=o_rowF, scalar=0.0, in1=o_t, op0=ALU.max, op1=ALU.add))
                then(V.tensor_scalar(o_t, o_t, gate_b[:, 5:6], None, ALU.mult))
                then(V.tensor_copy(o_rst.rearrange("p (c n) -> p c n", n=P), resets))
                then(V.tensor_tensor_scan(o_g[0:32], o_rst[0:32], o_t[0:32], 0.0, ALU.mult, ALU.add))
                then(V.tensor_tensor_scan(o_g[r][:, ::-1], o_rst[r][:, ::-1], o_t[r][:, ::-1], 0.0, ALU.mult, ALU.add))
                then(V.tensor_tensor(o_gb, o_gb, o_g, ALU.add))
                ends_of(o_g, endr[:, 0])
                V.memset(small[:, 7:8], 0.0).then_inc(sem("rows_diff1"), 1)
                dve.wait_ge(sem("rows_exp1"), 1)
                V.memset(small[:, 7:8], 0.0).then_inc(sem("rows_ready1"), 1)
                spread_ends(1, 0, endr[:, 0, 0:NT])
                dve.wait_ge(sem("columns_turned1"), 1)
                bykey(lambda d, s: then(V.tensor_scalar(cols[:, 3, :, d], turned(0, s), -1.0, None, ALU.mult)))
                bykey(lambda d, s: then(V.tensor_copy(cols[:, 1, :, d], turned(1, s))))
                then(V.tensor_tensor(cols[:, 0], cols[:, 3], cols[:, 1], ALU.add))
                dve.wait_ge(sem("ends_out1"), 1)
                bykey(lambda d, s: then(V.tensor_copy(endb[:, :, d], turned(2, s))))
                bykey(lambda d, s: V.tensor_tensor(cols[:, 2, :, d], cols[:, 3, :, d], turned(2, s), ALU.add).then_inc(sem("dn_wexp"), 1))

            def deltanet():
                dve.wait_ge(sem("dn_cols"), 1)
                streams = [Stream(d) for d in range(2)]
                eye = ident.unsqueeze(1).to_broadcast([P, 4, P])
                for i in range(STEPS):
                    lat = i - LAT_STEP
                    for d, st in enumerate(streams):
                        dve.wait_ge(sem("dn_aexp"), nth(i, d))
                        V.tensor_tensor(st.AT, st.X, st.ps(1), ALU.mult).then_inc(sem("dn_at"), 1)
                    if lat >= 0:
                        for d, st in enumerate(streams):
                            dve.wait_ge(sem("dn_qexp"), nth(lat, d))
                            V.tensor_tensor(st.ATTN, st.Y, st.ps(3), ALU.mult).then_inc(sem("dn_q"), 1)
                        for d, st in enumerate(streams):
                            dve.wait_ge(sem("dn_q_in"), nth(lat, d, 2, 1))
                            V.tensor_tensor(st.QG, proj[:, DNQ:DNQ + 4, st.tokens(i)], st.ps(0), ALU.mult).then_inc(sem("dn_q"), 1)
                    for d, st in enumerate(streams):
                        dve.wait_ge(sem("dn_y_in"), nth(i, d, LEVELS))
                        V.tensor_tensor(st.X, eye, st.ps(1), ALU.add).then_inc(sem("dn_x"), 1)
                        V.tensor_tensor(st.XT, eye, st.LV[0], ALU.add).then_inc(sem("dn_xt"), 1)
                    for k in range(1, LEVELS):
                        if k >= 2:
                            for d, st in enumerate(streams):
                                dve.wait_ge(sem("dn_t_in"), nth(i, d, LEVELS - 2, k - 2))
                                V.tensor_copy(st.XT, st.ps(3)).then_inc(sem("dn_xt"), 1)
                        for d, st in enumerate(streams):
                            dve.wait_ge(sem("dn_z_in"), nth(i, d, LEVELS - 1, k - 1))
                            if k < LEVELS - 1:
                                dve.wait_ge(sem("dn_x"), nth(i, d, LEVELS - 1, k - 1))
                                V.tensor_tensor(st.X, st.X, st.ps(2), ALU.add).then_inc(sem("dn_x"), 1)
                            else:
                                dve.wait_ge(sem("dn_xt"), nth(i, d, LEVELS, k - 1))
                                V.tensor_tensor(st.XT, st.XT, st.ps(2), ALU.add).then_inc(sem("dn_xt"), 1)
                    for d, st in enumerate(streams):
                        dve.wait_ge(sem("dn_u_in"), nth(i, d))
                        V.tensor_copy(st.U, st.ps(2)).then_inc(sem("dn_u"), 1)
                    for d, st in enumerate(streams):
                        c = st.chunk(i)
                        if lat >= 0:
                            dve.wait_ge(sem("dn_o_in"), nth(lat, d))
                            y = hT[:, 4:8, st.tokens(i)]
                            if 2 * lat < NT - LAT_STEP:
                                V.tensor_copy(y, st.ps(3)).then_inc(sem("dn_o"), 1)
                            else:
                                dve.wait_ge(sem("dn_o"), NT - LAT_STEP)
                                V.tensor_tensor(y, y, st.ps(3), ALU.add).then_inc(sem("dn_o"), 1)
                        dve.wait_ge(sem("dn_s_in"), nth(i, d))
                        if i == 0:
                            V.tensor_copy(st.ST, st.ps(0)).then_inc(sem("dn_state"), 1)
                        else:
                            dve.wait_ge(sem("dn_state"), nth(i - 1, d))
                            for h in range(HEADS):
                                last = V.scalar_tensor_tensor(out=st.ST[:, h, :], in0=st.ST[:, h, :], scalar=endb[:, c, 4 * d + h:4 * d + h + 1],
                                                              in1=st.head(0, h), op0=ALU.mult, op1=ALU.add)
                            last.then_inc(sem("dn_state"), 1)

            def gate_y(layer, first, c0, stage):
                for h in range(HEADS):
                    dve.wait_ge(sem("hnorm"), HEAD_BASE[stage] + h + 1)
                    dve.wait_ge(sem(f"out_gate{layer}"), h + 1)
                    V.tensor_tensor(hT[:, 4 + h, c0:T], hT[:, 4 + h, c0:T], proj[:, first + h, c0:T], ALU.mult).then_inc(sem(f"y_gated{layer}"), 1)

            def added(stage, layer, ga, c0, signal):
                j0, n, per, done = PLAN[f"{stage}{layer}"]
                if stage == "out":
                    for b in range(8):
                        dve.wait_ge(sem("products"), done + b + 1)
                        add_in(b, 2 * (b % 4), layer, ga, c0, signal)
                else:
                    with dve.Fori(0, 4) as i:
                        for b in range(2):
                            dve.wait_ge(sem("products"), 4 * i + (done + 2 * b + 2))
                            add_in(2 * i + b, 2 * b, layer, ga, c0, signal)

            def up(layer, c0):
                _, _, _, done = PLAN[f"up{layer}"]
                w = T - c0

                def body(f, i):
                    dve.wait_ge(sem("products"), 8 * i + (done + 4 * (f // 2) + 2 + f % 2 + 1))
                    dve.wait_ge(sem(f"ffn_silu{layer}"), 4 * i + (f + 1))
                    V.tensor_tensor(proj[:, bass.ds(4 * i + f, 1), c0:T].rearrange("p a t -> p (a t)"), sq[:, f % 2, 0:w],
                                    ps(4 + 2 * (f % 2), 0, w), ALU.mult).then_inc(sem(f"ffn_act{layer}"), 1)

                with dve.Fori(0, FC // 4) as i:
                    for f in range(4):
                        body(f, i)
                for f in range(FC % 4):
                    body(f, FC // 4)

            for layer in range(2):
                c0 = 0 if layer == 0 else CTX
                if layer == 0:
                    dve.wait_ge(sem("mod_ready"), 1)
                norm(f"mix{layer}", 0, gmT[:, layer, 0], modT[:, layer, SH1:SH1 + KD])
                project_out(layer)
                output = att_output(layer)
                if layer == 0:
                    for k in range(KD):
                        V.tensor_tensor(hT[:, k, :], h_hi[:, k, :], hT_lo[:, k, :], ALU.add).then_inc(sem("h_back"), 1)
                    gate_rows(0)
                    dve.wait_ge(sem("proj_moved0"), 24)
                    rope(0)
                    attention(0)
                    dve.wait_ge(sem("ada_turned"), 48)
                    modulation(16, 96, [(0, 1), (1, 0), (1, 1)])
                    rows_even()
                    mlstm()
                    unit_norm(2 * HEADS)
                    gate_y(0, MLO, 0, "ml")
                else:
                    dve.wait_ge(sem("proj_moved1"), 22)
                    head_norm("l2")
                    dve.wait_ge(sem("moved_odd"), 3 * NT)
                    gate_rows(1)
                    head_norm("qk")
                    dve.wait_ge(sem("hnorm"), HEAD_BASE["qk"] + 5)
                    rope(1)
                    attention(1)
                    rows_odd()
                    deltanet()
                    head_norm("dn")
                    gate_y(1, DNZ, CTX, "dn")
                for k in range(KD):
                    dve.wait_ge(sem("h_hi"), H_BASE[f"out{layer}"] + k + 1)
                    V.tensor_tensor(hT_lo[:, k, c0:T], hT[:, k, c0:T], h_hi[:, k, c0:T], ALU.subtract).then_inc(sem("h_ready"), 1)
                added("out", layer, GA1, c0, f"out_added{layer}")
                dve.wait_ge(sem(f"out_added{layer}"), 8 * (2 if c0 == 0 else 1))
                norm(f"ffn{layer}", c0, gmT[:, layer, 1], modT[:, layer, SH2:SH2 + KD])
                up(layer, c0)
                for k in range(DOWN_SPLIT):
                    dve.wait_ge(sem("h_hi"), H_BASE[f"down{layer}"] + k + 1)
                    V.tensor_tensor(proj_lo[:, k, c0:T], proj[:, k, c0:T], act_hi(k)[:, c0:T], ALU.subtract).then_inc(sem("h_ready"), 1)
                added("down", layer, GA2, c0, f"down_added{layer}")
                dve.wait_ge(sem(f"down_added{layer}"), 8 * (2 if c0 == 0 else 1))
            norm("final", CTX, None, None, vec_b[:, G_FINAL:G_FINAL + 8])


_INS = ["x", "c", "ctx", "c_ctx", "w_ada", "b_ada", "g_mix", "g_ffn", "w_in_e", "b_gate_e", "da_lam", "da_norm_g", "ml_norm_g",
        "w_out_e", "w_in_o", "qk_norm_g", "dn_conv", "dn_a_log", "dn_dt_bias", "dn_norm_g", "w_out_o", "w_gate", "w_up", "w_down",
        "g_final"]


def kernel(**inputs):
    import concourse.bacc as bacc
    from concourse.bass_utils import run_bass_kernel_spmd as run

    nc = bacc.Bacc("TRN2", target_bir_lowering=False, num_devices=1)
    arrays, args = {}, []
    tables = dict(zip(("const_f", "const_b", "rotary"), constant_tables()))
    for name in _INS + ["const_f", "const_b", "rotary"]:
        a = np.ascontiguousarray(inputs[name] if name in inputs else tables[name])
        arrays[f"in_{name}_dram"] = a
        args.append(nc.dram_tensor(f"in_{name}_dram", a.shape, mybir.dt.from_np(a.dtype), kind="ExternalInput").ap())
    args.append(nc.dram_tensor("out_0_dram", (1, LAT, D), F32, kind="ExternalOutput").ap())
    backbone(nc, *args)
    r = run(nc, [arrays], core_ids=[0])
    return r.results[0]["out_0_dram"]
```
